# Optimizing a Trainium2 kernel written in Bass

```python
import jax
import jax.numpy as jnp
from jax import lax
import numpy as np

D_MODEL = 1024
BATCH = 1
SEQ = 512
DEPTH = 2

N_MIXERS = 2
N_GLA_LAYERS = (DEPTH + 1) // 2
N_SGU_LAYERS = DEPTH // 2

GLA_HEADS = 4
GLA_DK = D_MODEL // 2
GLA_DV = D_MODEL
GLA_HK = GLA_DK // GLA_HEADS
GLA_HV = GLA_DV // GLA_HEADS
GLA_GATE_RANK = 16
GLA_TAU = 16.0
GLA_CHUNK = 64
GLA_IN = 2 * GLA_DK + 2 * GLA_DV + GLA_GATE_RANK

SGU_WIDTH = 2 * D_MODEL
SGU_GROUPS = 8
SGU_GC = SGU_WIDTH // SGU_GROUPS
SGU_CHUNK = 128

MOE_GROUPS = 4
MOE_EXPERTS_PER_GROUP = 4
MOE_N_EXPERTS = MOE_GROUPS * MOE_EXPERTS_PER_GROUP
MOE_TOP_K = 2
MOE_FF = D_MODEL // 2

PLE_DIM = 256
NORM_EPS = 1e-6

kernel_name = 'hybrid_gla_sgu_hmoe_ple'

def rms_norm(x, g):
    xf = x.astype(jnp.float32)
    y = xf * lax.rsqrt(jnp.mean(xf * xf, axis=-1, keepdims=True) + NORM_EPS)
    return (y * g.astype(jnp.float32)).astype(x.dtype)

def layer_norm(x, g, b):
    xf = x.astype(jnp.float32)
    xc = xf - jnp.mean(xf, axis=-1, keepdims=True)
    y = xc * lax.rsqrt(jnp.mean(xc * xc, axis=-1, keepdims=True) + NORM_EPS)
    return (y * g.astype(jnp.float32) + b.astype(jnp.float32)).astype(x.dtype)

def gla_mixer(h, w_in, w_gate_up, b_gate, g_head, w_out):
    B, S, _ = h.shape
    nc = S // GLA_CHUNK
    z = h @ w_in
    q, k, v, r, a = jnp.split(
        z, [GLA_DK, 2 * GLA_DK, 2 * GLA_DK + GLA_DV, 2 * GLA_DK + 2 * GLA_DV], axis=-1)
    log_alpha = jax.nn.log_sigmoid((a @ w_gate_up + b_gate).astype(jnp.float32)) / GLA_TAU

    def heads(t, dh):
        return t.astype(jnp.float32).reshape(B, nc, GLA_CHUNK, GLA_HEADS, dh).transpose(0, 3, 1, 2, 4)

    q = heads(q, GLA_HK) * (GLA_HK ** -0.5)
    k = heads(k, GLA_HK)
    v = heads(v, GLA_HV)
    bcum = jnp.cumsum(heads(log_alpha, GLA_HK), axis=3)
    b_end = bcum[:, :, :, -1, :]
    q_dec = q * jnp.exp(bcum)
    k_dec = k * jnp.exp(-bcum)
    causal = jnp.tril(jnp.ones((GLA_CHUNK, GLA_CHUNK), dtype=bool))
    attn = jnp.where(causal, jnp.einsum('bhnik,bhnjk->bhnij', q_dec, k_dec), 0.0)
    o_intra = jnp.einsum('bhnij,bhnjv->bhniv', attn, v)
    k_end = k * jnp.exp(b_end[:, :, :, None, :] - bcum)
    chunk_kv = jnp.einsum('bhnjk,bhnjv->bhnkv', k_end, v)

    def step(state, inp):
        decay, kv = inp
        return decay[..., None] * state + kv, state

    s0 = jnp.zeros((B, GLA_HEADS, GLA_HK, GLA_HV), jnp.float32)
    _, states = lax.scan(step, s0, (jnp.moveaxis(jnp.exp(b_end), 2, 0), jnp.moveaxis(chunk_kv, 2, 0)))
    states = jnp.moveaxis(states, 0, 2)
    o = o_intra + jnp.einsum('bhnik,bhnkv->bhniv', q_dec, states)
    o = o.transpose(0, 2, 3, 1, 4).reshape(B, S, GLA_HEADS, GLA_HV)
    o = rms_norm(o, g_head.reshape(GLA_HEADS, GLA_HV)).reshape(B, S, GLA_DV)
    o = jax.nn.silu(r.astype(jnp.float32)) * o
    return o.astype(h.dtype) @ w_out

def sgu_mixer(h, w_in, ln_g, ln_b, w_s, b_s, w_out):
    B, S, _ = h.shape
    nc = S // SGU_CHUNK
    z = jax.nn.gelu(h @ w_in)
    u, v = jnp.split(z, 2, axis=-1)
    v = layer_norm(v, ln_g, ln_b).reshape(B, nc, SGU_CHUNK, SGU_GROUPS, SGU_GC)
    causal = jnp.tril(jnp.ones((SGU_CHUNK, SGU_CHUNK), dtype=bool))
    w_causal = jnp.where(causal, w_s, 0.0)
    s = jnp.einsum('gts,bnsgc->bntgc', w_causal, v) + jnp.transpose(b_s)[None, None, :, :, None]
    return (u * s.reshape(B, S, SGU_WIDTH)) @ w_out

def hier_moe(h, w_rg, b_rg, w_re, b_re, w_gate, w_up, w_down):
    f32 = jnp.float32
    group_logits = (h @ w_rg + b_rg).astype(f32)
    group_probs = jax.nn.softmax(group_logits, axis=-1)
    g_idx = jnp.argmax(group_logits, axis=-1)
    g_w = jnp.take_along_axis(group_probs, g_idx[..., None], axis=-1)
    expert_logits = (jnp.einsum('bsd,dge->bsge', h, w_re) + b_re).astype(f32)
    in_group = jnp.take_along_axis(expert_logits, g_idx[..., None, None], axis=2)[:, :, 0, :]
    top_vals, top_idx = lax.top_k(in_group, MOE_TOP_K)
    top_w = jax.nn.softmax(top_vals, axis=-1) * g_w
    expert_id = g_idx[..., None] * MOE_EXPERTS_PER_GROUP + top_idx
    combine = jnp.sum(jax.nn.one_hot(expert_id, MOE_N_EXPERTS, dtype=f32) * top_w[..., None],
                      axis=-2).astype(h.dtype)

    def per_row(args):
        hb, cb = args
        a = jnp.einsum('sd,edf->sef', hb, w_gate)
        b = jnp.einsum('sd,edf->sef', hb, w_up)
        act = jax.nn.silu(a) * b * cb[:, :, None]
        return jnp.einsum('sef,efd->sd', act, w_down)

    return lax.map(per_row, (h, combine))

def per_layer_embedding(hn, p_i, w_up, w_gate):
    return (p_i @ w_up) * jax.nn.sigmoid(hn @ w_gate)

def setup_inputs(seed: int = 0) -> dict:
    key = jax.random.key(seed)
    ks = jax.random.split(key, 26)

    def nrm(k, shape, scale):
        return jax.random.normal(k, shape, jnp.float32) * scale

    def gain(k, shape):
        return 1.0 + 0.02 * jax.random.normal(k, shape, jnp.float32)

    NA, NB, L, D = N_GLA_LAYERS, N_SGU_LAYERS, DEPTH, D_MODEL
    return {
        'x': nrm(ks[0], (BATCH, SEQ, D), 1.0),
        'p': nrm(ks[1], (DEPTH, BATCH, SEQ, PLE_DIM), 1.0),
        'gla_w_in': nrm(ks[2], (NA, D, GLA_IN), D ** -0.5),
        'gla_w_gate_up': nrm(ks[3], (NA, GLA_GATE_RANK, GLA_DK), GLA_GATE_RANK ** -0.5),
        'gla_b_gate': nrm(ks[4], (NA, GLA_DK), 0.1),
        'gla_g_head': gain(ks[5], (NA, GLA_DV)),
        'gla_w_out': nrm(ks[6], (NA, GLA_DV, D), GLA_DV ** -0.5),
        'sgu_w_in': nrm(ks[7], (NB, D, 2 * SGU_WIDTH), D ** -0.5),
        'sgu_ln_g': gain(ks[8], (NB, SGU_WIDTH)),
        'sgu_ln_b': nrm(ks[9], (NB, SGU_WIDTH), 0.02),
        'sgu_w_s': nrm(ks[10], (NB, SGU_GROUPS, SGU_CHUNK, SGU_CHUNK), 0.5 * SGU_CHUNK ** -0.5),
        'sgu_b_s': gain(ks[11], (NB, SGU_GROUPS, SGU_CHUNK)),
        'sgu_w_out': nrm(ks[12], (NB, SGU_WIDTH, D), SGU_WIDTH ** -0.5),
        'norm_mix_g': gain(ks[13], (L, D)),
        'norm_ffn_g': gain(ks[14], (L, D)),
        'norm_ple_g': gain(ks[15], (L, D)),
        'moe_w_route_group': nrm(ks[16], (L, D, MOE_GROUPS), D ** -0.5),
        'moe_b_route_group': nrm(ks[17], (L, MOE_GROUPS), 0.01),
        'moe_w_route_expert': nrm(ks[18], (L, D, MOE_GROUPS, MOE_EXPERTS_PER_GROUP), D ** -0.5),
        'moe_b_route_expert': nrm(ks[19], (L, MOE_GROUPS, MOE_EXPERTS_PER_GROUP), 0.01),
        'moe_w_gate': nrm(ks[20], (L, MOE_N_EXPERTS, D, MOE_FF), D ** -0.5),
        'moe_w_up': nrm(ks[21], (L, MOE_N_EXPERTS, D, MOE_FF), D ** -0.5),
        'moe_w_down': nrm(ks[22], (L, MOE_N_EXPERTS, MOE_FF, D), MOE_FF ** -0.5),
        'ple_w_up': nrm(ks[23], (L, PLE_DIM, D), PLE_DIM ** -0.5),
        'ple_w_gate': nrm(ks[24], (L, D, D), D ** -0.5),
        'final_norm_g': gain(ks[25], (D,)),
    }

def reference(x, p, gla_w_in, gla_w_gate_up, gla_b_gate, gla_g_head, gla_w_out,
              sgu_w_in, sgu_ln_g, sgu_ln_b, sgu_w_s, sgu_b_s, sgu_w_out,
              norm_mix_g, norm_ffn_g, norm_ple_g,
              moe_w_route_group, moe_b_route_group, moe_w_route_expert, moe_b_route_expert,
              moe_w_gate, moe_w_up, moe_w_down,
              ple_w_up, ple_w_gate, final_norm_g):
    h = x
    for i in range(DEPTH):
        j = i // N_MIXERS
        hn = rms_norm(h, norm_mix_g[i])
        if i % N_MIXERS == 0:
            h = h + gla_mixer(hn, gla_w_in[j], gla_w_gate_up[j], gla_b_gate[j],
                              gla_g_head[j], gla_w_out[j])
        else:
            h = h + sgu_mixer(hn, sgu_w_in[j], sgu_ln_g[j], sgu_ln_b[j],
                              sgu_w_s[j], sgu_b_s[j], sgu_w_out[j])
        h = h + hier_moe(rms_norm(h, norm_ffn_g[i]), moe_w_route_group[i], moe_b_route_group[i],
                         moe_w_route_expert[i], moe_b_route_expert[i],
                         moe_w_gate[i], moe_w_up[i], moe_w_down[i])
        h = h + per_layer_embedding(rms_norm(h, norm_ple_g[i]), p[i], ple_w_up[i], ple_w_gate[i])
    return rms_norm(h, final_norm_g)


_drawn_inputs = setup_inputs


def setup_inputs(seed=0):
    import zlib

    import numpy as np

    out = dict(_drawn_inputs(seed))
    spreads = {}
    factors = {'gla_g_head': 2.861,
     'sgu_ln_g': 47.367,
     'sgu_ln_b': 52.59,
     'sgu_b_s': 20.109,
     'norm_ple_g': 44.892,
     'moe_b_route_group': 27.298,
     'moe_b_route_expert': 15.216,
     'final_norm_g': 7.861,
     'norm_ffn_g': 3.085}
    for name, (base, spread) in spreads.items():
        noise = np.random.default_rng([zlib.crc32(name.encode()), seed]).standard_normal(out[name].shape)
        drawn = base * np.exp(spread * noise) if base else spread * noise
        out[name] = jnp.asarray(drawn.astype(out[name].dtype))
    for name, factor in factors.items():
        out[name] = (out[name] * factor).astype(out[name].dtype)
    return out
```

```python
from contextlib import ExitStack

import concourse.bass as bass
from concourse import mybir

F32 = mybir.dt.float32
F32R = mybir.dt.float32r
I32 = mybir.dt.int32
ACT = mybir.ActivationFunctionType
ALU = mybir.AluOpType
AX = mybir.AxisListType

P = 128
D = 1024
SEQ = 512
NT = SEQ // P
KD = D // P
UNIT = 2048
RAW = 3
SPLIT = 3
AHEAD = SPLIT - 1
HEADS = 4
HV = D // HEADS
CHUNK = 64
TAU = 16.0
EXPERTS = 16
PER_EXPERT = 6
EPS = 1e-6
BIG = 1 << 20
ROUNDS = SEQ // P
SLOTS = P * ROUNDS * EXPERTS
FAR = -3.0e38

V0, Q, K, V1, R0, R1, GO0, GO1 = range(0, 16, 2)
UP = [16, 141]
MOE = [17, 142]
PG = [113, 238]
SV = [117 + 2 * c for c in range(4)]
SU = [125 + 2 * c for c in range(4)]
SO = [[133, 135], [137, 139]]
UNITS = 242
MISC = 16 * 7

C_ID, C_ONE, C_BEFORE, C_CHUNK, C_CAUSAL, C_TIE, C_EOFF = 0, 128, 256, 384, 512, 640, 656
C_END = C_EOFF + 64
S_BG, S_BS, S_RB = 0, 4, 12
S_END = 12 + 160


def unit_of(layer, i, j):
    return MOE[layer] + (j if isinstance(i, int) and i == 0 else PER_EXPERT * i - 2 + j)


def build(nc, weight_stream, x_in, consts_in, ids_in, scan_in, small_in, gains_in, ln_in, router_in, wa_in, wgu_in, ws_in,
          pt_in, out, hn_dram, y_dram, list_dram):
    stack = ExitStack()
    with stack:
        def sb(name, shape, dt=F32, on=None):
            return (on or stack).enter_context(nc.sbuf_tensor(name, shape, dt))

        def sem(name):
            return stack.enter_context(nc.semaphore(name))

        raw = sb("raw", [P, RAW, UNIT])
        WH = sb("WH", [P, SPLIT, UNIT], F32R)
        WL = sb("WL", [P, SPLIT, UNIT], F32R)
        XTH = sb("XTH", [P, KD, SEQ], F32R)
        XTL = sb("XTL", [P, KD, SEQ], F32R)
        H = sb("H", [P, NT, D])
        HN = sb("HN", [P, 2, D])
        gain = sb("gain", [P, D])
        con = sb("con", [P, C_END])
        ids = sb("ids", [P, 2 * NT], I32)
        small = sb("small", [P, S_END])
        RWH = sb("RWH", [P, 2, KD, 20], F32R)
        RWL = sb("RWL", [P, 2, KD, 20], F32R)
        square_sum = sb("square_sum", [P, NT])
        root = sb("root", [P, NT])
        rstd = sb("rstd", [P, NT])
        w_tok = sb("w_tok", [P, 2, NT])
        slot_rows = sb("slot_rows", [P, ROUNDS * EXPERTS], I32)
        slot_tokens = sb("slot_tokens", [P, ROUNDS * EXPERTS], I32)
        gather_col = sb("gather_col", [P, 1], I32)
        scatter_col = sb("scatter_col", [P, 1], I32)
        empty = sb("empty", [P, ROUNDS * EXPERTS], I32)
        rounds_i = sb("rounds_i", [P, 1], I32)

        ident = con[:, C_ID:C_ID + P]
        ones = con[:, C_ONE:C_ONE + P]
        before = con[:, C_BEFORE:C_BEFORE + P]
        chunk_mask = con[:, C_CHUNK:C_CHUNK + P]
        causal = con[:, C_CAUSAL:C_CAUSAL + P]
        tie = con[:, C_TIE:C_TIE + 16].rearrange("p (t e) -> p t e", t=NT)
        eoff = con[:, C_EOFF:C_EOFF + 64].rearrange("p (t e) -> p t e", t=NT)

        with ExitStack() as r1:
            E1 = sb("E1", [P, HEADS, SEQ], on=r1)
            E2 = sb("E2", [P, HEADS, SEQ], on=r1)
            E3 = sb("E3", [P, HEADS, SEQ], on=r1)
            VG = sb("VG", [P, NT, D], on=r1)
            SR = sb("SR", [P, NT, D], on=r1)
            bcum = sb("bcum", [P, 2, SEQ], on=r1)
            chunk_decay = sb("chunk_decay", [P, HEADS, SEQ // CHUNK], on=r1)
            oss = sb("oss", [P, 3, HEADS], on=r1)
            o_junk = sb("o_junk", [P, HV], on=r1)
        with ExitStack() as r1b:
            sb("skip_E", [P, 3, HEADS * SEQ], on=r1b)
            WAH = sb("WAH", [P, KD, P], F32R, on=r1b)
            WAL = sb("WAL", [P, KD, P], F32R, on=r1b)
            sb("skip_SR", [P, 2 * D], on=r1b)
            WGU = sb("WGU", [P, 4 * P], on=r1b)
            aT = sb("aT", [P, SEQ], on=r1b)
            rwa = sb("rwa", [P, KD, P], on=r1b)
            rwr = sb("rwr", [P, 2, KD, 20], on=r1b)
            scan_mask = sb("scan_mask", [P, SEQ], on=r1b)
        with ExitStack() as r2:
            VS = sb("VS", [P, NT, 2 * D], on=r2)
            UT = sb("UT", [P, NT, 512], on=r2)
            WST = sb("WST", [P, 8, P], on=r2)
            lnG = sb("lnG", [P, D], on=r2)
            lnB = sb("lnB", [P, D], on=r2)
            vsum = sb("vsum", [P, NT, 4], on=r2)
            vst = sb("vst", [P, 5, NT], on=r2)
        with ExitStack() as r3:
            PU = sb("PU", [P, NT, D], on=r3)
            junk3 = sb("junk3", [P, D], on=r3)
            pT = sb("pT", [P, 2, SEQ], on=r3)
            pTH = sb("pTH", [P, 2, SEQ], F32R, on=r3)
            pTL = sb("pTL", [P, 2, SEQ], F32R, on=r3)
            with ExitStack() as r3e:
                XG = sb("XG", [P, D], on=r3e)
                SG = sb("SG", [P, 512], on=r3e)
                AG = sb("AG", [P, 512], on=r3e)
                ATH = sb("ATH", [P, 4, P], F32R, on=r3e)
                ATL = sb("ATL", [P, 4, P], F32R, on=r3e)
                Y = sb("Y", [P, D], on=r3e)
            Y2 = sb("Y2", [P, 2, 2 * D], on=r3)
            lg = sb("lg", [P, NT, 20], on=r3)
            r4 = sb("r4", [P, 12, NT, 4], on=r3)
            r16 = sb("r16", [P, 6, NT, 16], on=r3)
            r1t = sb("r1t", [P, 12, NT], on=r3)
            pos_f = sb("pos_f", [P, 2, NT], on=r3)
            pos_i = sb("pos_i", [P, 2 * NT], I32, on=r3)
            cnt = sb("cnt", [P, 4], on=r3)
        XO = HN[:, 0, :].rearrange("p (k s) -> p k s", k=KD)
        AO = HN[:, 1, 0:512].rearrange("p (k s) -> p k s", k=4)
        with ExitStack() as r3o:
            sb("skip_PU", [P, NT * D], on=r3o)
            WOV = sb("WOV", [P, UNIT], on=r3o)
        GT = Y2[:, 0:1, :].rearrange("p a (j n) -> p (a j) n", j=NT)
        AS = bcum[:, :, :].rearrange("p b (h i) -> p b h i", h=HEADS)
        ST = HN[:, :, :].rearrange("p b (h v) -> p b h v", h=HEADS)

        ps = [stack.enter_context(nc.psum_tensor(f"bank{i}", [P, 512], F32)) for i in range(8)]

        raw_loaded = [sem(f"raw_loaded{i}") for i in range(RAW)]
        S = {n: sem(n) for n in (
            "hi_ready lo_ready unit_used x_loaded misc_loaded gain_loaded ln_loaded pt_loaded list_cleared "
            "rows_ready rms_ready xt_pe xt_hi xt_lo tile_done freed_act freed_dve early_split_hi early_split_lo "
            "a_done a_copied z_done z_read abs_read decay_act bc_ready dlt_ready e_ready kt_done kt_copied sr_scaled "
            "score_done mask_done kv_done state_ready o_done o_root o_gated act_chain dve_chain pool_chain up_done "
            "router_done exp_in exp_out mask16_ready rank_done routed slots_written slots_loaded slots_ready "
            "pt_hi pt_lo at_pe at_hi at_lo gx_pe gx_hi gx_lo silu_ready glu_ready y_act y_dve gathered scattered "
            "col_copied combined ple_added ln_root ln_done mean_ready s_done prod_done ws_loaded ws_masked "
            "out_ready out_stored").split()}

        hn_stored = [sem(f"hn_stored{b}") for b in range(2)]
        y_loaded = [sem(f"y_loaded{b}") for b in range(2)]
        OV = [{n: sem(f"ov{layer}_{n}") for n in (
            "gathered scattered weights used x_pe x_copied silu glu a_pe a_copied y col".split())} for layer in range(2)]

        act_blocks = ["v0", "v1", "r0", "r1", "up00", "up01", "pg00", "pg01", "sv0", "sv1", "sv2", "sv3",
                      "su0", "su1", "su2", "su3", "up10", "up11", "pg10", "pg11"]
        dve_blocks = ["q", "k", "go0", "go1", "so00", "so01", "so10", "so11"]

        def wait_freed(eng, block, j):
            if block in act_blocks:
                eng.wait_ge(S["freed_act"], 4 * act_blocks.index(block) + j + 1)
            else:
                eng.wait_ge(S["freed_dve"], 4 * dve_blocks.index(block) + j + 1)

        dense_order = ["v0", "q", "k", "v1", "r0", "r1", "go0", "go1", "pg00", "pg01", "sv0", "sv1", "sv2", "sv3",
                       "su0", "su1", "su2", "su3", "so00", "so01", "so10", "so11", "pg10", "pg11"]

        def wait_tile(eng, block, last_unit, j):
            if j < 3:
                eng.wait_ge(S["tile_done"], 3 * dense_order.index(block) + j + 1)
            else:
                eng.wait_ge(S["unit_used"], last_unit + 1)

        def mm3(pe, dst, ah, al, bh, bl, start, stop):
            pe.matmul(dst, ah, bh, start=start, stop=False)
            pe.matmul(dst, ah, bl, start=False, stop=False)
            return pe.matmul(dst, al, bh, start=False, stop=stop)

        block = stack.enter_context(nc.Block())

        @block.sync
        def _(sp):
            sp.dma_start(H[:, :, :], x_in).then_inc(S["x_loaded"], 16)
            sp.dma_start(con[:, :], consts_in).then_inc(S["misc_loaded"], 16)
            sp.dma_start(ids[:, :], ids_in).then_inc(S["misc_loaded"], 16)
            sp.dma_start(small[:, :], small_in).then_inc(S["misc_loaded"], 16)
            sp.dma_start(rwr[:, :, :, :], router_in).then_inc(S["misc_loaded"], 16)
            sp.dma_start(rwa[:, :, :], wa_in).then_inc(S["misc_loaded"], 16)
            sp.dma_start(scan_mask[:, :], scan_in).then_inc(S["misc_loaded"], 16)
            sp.dma_start(WGU[:, :], wgu_in).then_inc(S["misc_loaded"], 16)
            for u in range(RAW):
                sp.dma_start(raw[:, u, :], weight_stream[u]).then_inc(raw_loaded[u], 16)
            turns = UNITS // RAW
            with sp.Fori(1, turns) as n:
                for s in range(RAW):
                    src = weight_stream[bass.ds(n * RAW + s, 1)].rearrange("u p f -> p (u f)")
                    sp.wait_ge(S["lo_ready"], n * RAW + s - RAW + 1)
                    sp.dma_start(raw[:, s, :], src).then_inc(raw_loaded[s], 16)
            for u in range(turns * RAW, UNITS):
                sp.wait_ge(S["lo_ready"], u - RAW + 1)
                sp.dma_start(raw[:, u % RAW, :], weight_stream[u]).then_inc(raw_loaded[u % RAW], 16)
            for t in range(NT):
                sp.wait_ge(S["out_ready"], t + 1)
                sp.dma_start(out[t], H[:, t, :]).then_inc(S["out_stored"], 16)
            sp.wait_ge(S["out_stored"], 16 * NT)

        class Splitter:

            def __init__(self, eng, high):
                self.eng, self.high, self.next = eng, high, 0

            def one(self, u, slot_of):
                rs, ss = slot_of % RAW, slot_of % SPLIT
                if self.high:
                    self.eng.wait_ge(raw_loaded[rs], (u - rs) // RAW * 16 + 16 if isinstance(u, int) else self.turn(u, slot_of))
                    if not isinstance(u, int) or u >= SPLIT:
                        self.eng.wait_ge(S["unit_used"], u - SPLIT + 1)
                    self.eng.activation(WH[:, ss, :], raw[:, rs, :], ACT.Copy).then_inc(S["hi_ready"], 1)
                else:
                    self.eng.wait_ge(S["hi_ready"], u + 1)
                    self.eng.tensor_tensor(WL[:, ss, :], raw[:, rs, :], WH[:, ss, :], ALU.subtract)\
                        .then_inc(S["lo_ready"], 1)

            def turn(self, u, slot_of):
                return (PER_EXPERT // RAW * self.i + slot_of // RAW) * 16 + 16

            def to(self, u_last):
                while self.next <= min(u_last, UNITS - 1):
                    self.one(self.next, self.next)
                    self.next += 1

            def to_in_loop(self, layer, i, j_last):
                self.i = i
                while self.next <= j_last + AHEAD:
                    at0 = MOE[layer] - 2 + self.next
                    self.one(PER_EXPERT * i + at0, at0)
                    self.next += 1

        LOOP = (2, 14)

        def moe_steps(eng, layer, split, step):
            for i in range(LOOP[0]):
                step(i, (lambda j, i=i: split.to(unit_of(layer, i, j) + AHEAD)) if split else None)
            if split:
                split.to(unit_of(layer, LOOP[0], -1) + AHEAD)
                assert split.next == unit_of(layer, LOOP[0], 0) + AHEAD
                split.next = AHEAD
            with eng.Fori(*LOOP) as i:
                step(i, (lambda j: split.to_in_loop(layer, i, j)) if split else None)
                if split:
                    split.to_in_loop(layer, i, 5)
            if split:
                split.next = unit_of(layer, LOOP[1], 0) + AHEAD
            for i in range(LOOP[1], EXPERTS + 2):
                step(i, (lambda j, i=i: split.to(unit_of(layer, i, j) + AHEAD)) if split else None)

        def last_down(layer, e):
            return unit_of(layer, e + 1, 1 if isinstance(e, int) and e == EXPERTS - 1 else 5)

        def y_free(eng, q, i):
            eng.wait_ge(S["scattered"], 16 * q)

        def has(i, lo, hi):
            return not isinstance(i, int) or lo <= i <= hi

        def overflow(eng, layer, body):
            rounds = eng.value_load(rounds_i[0:1, 0:1], min_val=1, max_val=ROUNDS)
            with eng.If(rounds > 1):
                with eng.Fori(1, rounds) as r:
                    with eng.Fori(0, EXPERTS) as e:
                        body((r - 1) * EXPERTS + e, OV[layer])

        @block.tensor
        def _(pe):
            def transposes(n, base, source, ready):
                for t in range(NT):
                    ready(t)
                    for half in range(2):
                        bank = ps[base + 2 * (t % 2) + half]
                        if t >= 2:
                            pe.wait_ge(S["xt_lo"], 8 * n + 2 * (t - 2) + half + 1)
                        for q in range(4):
                            last = pe.transpose(bank[:, q * P:(q + 1) * P], source(t, 4 * half + q), ident)
                        last.then_inc(S["xt_pe"], 1)

            def rows(n):
                return lambda t: pe.wait_ge(S["rows_ready"], 4 * n + t + 1)

            def hn(t, k):
                return HN[:, t % 2, k * P:(k + 1) * P]

            def dense(name, u0, base, n_xt, free, feature_major=False):
                for half in range(2):
                    u = u0 + half
                    s = u % SPLIT
                    pe.wait_ge(S["lo_ready"], u + 1)
                    if feature_major and half == 0:
                        pe.wait_ge(S["xt_lo"], 8 * n_xt + 8)
                    for j in range(4):
                        if half == 0:
                            free(j)
                            if not feature_major:
                                pe.wait_ge(S["xt_lo"], 8 * n_xt + 2 * j + 2)
                        for k in range(4):
                            kk = 4 * half + k
                            start, stop = half == 0 and k == 0, half == 1 and k == 3
                            if feature_major:
                                c = slice(k * 512 + j * P, k * 512 + (j + 1) * P)
                                last = mm3(pe, ps[base + j][:, :], WH[:, s, c], WL[:, s, c],
                                           XTH[:, kk, :], XTL[:, kk, :], start, stop)
                            else:
                                c, r = slice(k * 512, (k + 1) * 512), slice(j * P, (j + 1) * P)
                                last = mm3(pe, ps[base + j][:, :], XTH[:, kk, r], XTL[:, kk, r],
                                           WH[:, s, c], WL[:, s, c], start, stop)
                        if j == 3:
                            last.then_inc(S["unit_used"], 1)
                        elif half == 1:
                            last.then_inc(S["tile_done"], 1)

            def xt_free(n):
                return lambda j: pe.wait_ge(S["xt_lo"], 8 * n + 4 + 2 * (j // 2) + j % 2 + 1)

            def after(name):
                return lambda j: wait_freed(pe, name, j)

            pe.wait_ge(S["misc_loaded"], MISC)
            transposes(0, 0, hn, rows(0))
            pe.wait_ge(S["xt_lo"], 8)
            pe.wait_ge(S["early_split_lo"], 2)
            for k in range(KD):
                last = mm3(pe, ps[4][:, :], WAH[:, k, :], WAL[:, k, :], XTH[:, k, :], XTL[:, k, :],
                           k == 0, k == KD - 1)
            last.then_inc(S["a_done"], 1)
            dense("v0", V0, 0, 0, xt_free(0))
            pe.wait_ge(S["a_copied"], 1)
            for h in range(HEADS):
                pe.matmul(ps[4 + h][:, :], WGU[:, h * P:(h + 1) * P], aT[:, :], start=True, stop=True)\
                    .then_inc(S["z_done"], 1)
            dense("q", Q, 0, 0, after("v0"), True)
            pe.wait_ge(S["z_read"], HEADS)
            dense("k", K, 4, 0, lambda j: None, True)
            dense("v1", V1, 0, 0, after("q"))
            dense("r0", R0, 4, 0, after("k"))
            dense("r1", R1, 0, 0, after("v1"))

            wait_freed(pe, "k", HEADS - 1)
            for t in range(NT):
                wait_freed(pe, "r0", t)
                for h in range(HEADS):
                    last = pe.transpose(ps[4 + t][:, h * P:(h + 1) * P], E3[:, h, t * P:(t + 1) * P], ident)
                last.then_inc(S["kt_done"], 1)
            KT = E3[:, :, :].rearrange("p h s -> p (h s)").rearrange("p (t h k) -> p t h k", t=NT, h=HEADS)
            for j in range(4):
                wait_freed(pe, "r1", j)

            def scores(t):
                bank = ps[t % 2]
                if t >= 2:
                    pe.wait_ge(S["mask_done"], t - 1)
                for h in range(HEADS):
                    last = pe.matmul(bank[:, h * P:(h + 1) * P], E2[:, h, t * P:(t + 1) * P],
                                     E1[:, h, t * P:(t + 1) * P], start=True, stop=True)
                last.then_inc(S["score_done"], 1)

            scores(0)
            pe.wait_ge(S["kt_copied"], NT)
            for t in range(NT):
                ob = 2 if t % 2 == 0 else 6
                if t + 1 < NT:
                    scores(t + 1)
                for c in range(2):
                    n = 2 * t + c
                    if n == SEQ // CHUNK - 1:
                        break
                    rows_c = slice(CHUNK * c, CHUNK * (c + 1))
                    if n >= 1:
                        pe.wait_ge(S["state_ready"], n)
                    for h in range(HEADS):
                        last = pe.matmul(ps[4 + h // 2][:, (h % 2) * HV:(h % 2 + 1) * HV], KT[rows_c, t, h, :],
                                         VG[rows_c, t, h * HV:(h + 1) * HV], start=True, stop=True)
                    last.then_inc(S["kv_done"], 1)
                pe.wait_ge(S["mask_done"], t + 1)
                if t >= 2:
                    pe.wait_ge(S["o_gated"], t - 1)
                pe.wait_ge(S["state_ready"], 2 * t + 1)
                for h in range(HEADS):
                    dst = ps[ob + h // 2][:, (h % 2) * HV:(h % 2 + 1) * HV]
                    last = pe.matmul(dst, AS[:, t % 2, h, :], VG[:, t, h * HV:(h + 1) * HV], start=True, stop=False,
                                     skip_group_check=True)
                    for c in range(2):
                        n = 2 * t + c
                        if n == 0:
                            continue
                        last = pe.matmul(dst[CHUNK * c:CHUNK * (c + 1), :],
                                         E1[:, h, n * CHUNK:(n + 1) * CHUNK], ST[:, n % 2, h, :],
                                         start=False, stop=c == 1, skip_group_check=True)
                last.then_inc(S["o_done"], 1)

            transposes(1, 0, lambda t, k: SR[:, t, k * P:(k + 1) * P],
                       lambda t: pe.wait_ge(S["o_gated"], max(t + 1, 3 if t == 1 else 0)))
            dense("go0", GO0, 4, 1, lambda j: None)
            dense("go1", GO1, 0, 1, xt_free(1))

            def router(layer, n_xt):
                pe.wait_ge(S["early_split_lo"], 2)
                pe.wait_ge(S["xt_lo"], 8 * n_xt + 8)
                for t in range(NT):
                    for k in range(KD):
                        last = mm3(pe, ps[6][:, t * 20:(t + 1) * 20], XTH[:, k, t * P:(t + 1) * P],
                                   XTL[:, k, t * P:(t + 1) * P], RWH[:, layer, k, :], RWL[:, layer, k, :],
                                   k == 0, k == KD - 1)
                last.then_inc(S["router_done"], 1)
                u = UP[layer]
                pe.wait_ge(S["pt_lo"], layer + 1)
                pe.wait_ge(S["lo_ready"], u + 1)
                for c in range(2):
                    for t in range(NT):
                        if c == 1:
                            wait_freed(pe, f"up{layer}0", t)
                        for k in range(2):
                            cols = slice(k * D + c * 512, k * D + (c + 1) * 512)
                            last = mm3(pe, ps[t][:, :], pTH[:, k, t * P:(t + 1) * P], pTL[:, k, t * P:(t + 1) * P],
                                       WH[:, u % SPLIT, cols], WL[:, u % SPLIT, cols], k == 0, k == 1)
                        if c == 1 and t == NT - 1:
                            last.then_inc(S["unit_used"], 1)
                        else:
                            last.then_inc(S["up_done"], 1)
                pe.wait_ge(S["mask16_ready"], layer + 1)
                M = r16[:, 2, :, :]
                for t in range(NT):
                    for b in range(t):
                        pe.matmul(ps[7][:, t * 16:(t + 1) * 16], ones, M[:, b, :], start=b == 0, stop=False)
                    pe.matmul(ps[7][:, t * 16:(t + 1) * 16], before, M[:, t, :], start=t == 0, stop=True)
                for t in range(NT):
                    last = pe.matmul(ps[7][:, 64:80], ones, M[:, t, :], start=t == 0, stop=t == NT - 1)
                last.then_inc(S["rank_done"], 1)
                for t in range(NT):
                    wait_freed(pe, f"up{layer}1", t)

            def gather_transposes(layer, e):
                q = EXPERTS * layer + e
                pe.wait_ge(S["gathered"], 16 * q + 16)
                for half in range(2):
                    if has(e, 1, 99) or layer:
                        pe.wait_ge(S["gx_lo"], 2 * q - 1 + half)
                    for k in range(4):
                        last = pe.transpose(ps[4 + half][:, k * P:(k + 1) * P],
                                            XG[:, (4 * half + k) * P:(4 * half + k + 1) * P], ident)
                    last.then_inc(S["gx_pe"], 1)

            def moe(layer):
                def step(i, _):
                    q = EXPERTS * layer + i
                    u = lambda j: unit_of(layer, i, j)
                    s0 = MOE[layer] + (0 if isinstance(i, int) and i == 0 else -2)
                    if has(i, 0, 0) and isinstance(i, int):
                        gather_transposes(layer, 0)
                    for which in range(2):
                        if has(i, 0, EXPERTS - 1):
                            if not (isinstance(i, int) and i == 0):
                                pe.wait_ge(S["silu_ready" if which == 0 else "glu_ready"], q)
                            if which == 0:
                                pe.wait_ge(S["gx_lo"], 2 * q + 2)
                            for half in range(2):
                                j = 2 * which + half
                                s = (s0 + j) % SPLIT
                                pe.wait_ge(S["lo_ready"], u(j) + 1)
                                for k in range(4):
                                    c = slice(k * 512, (k + 1) * 512)
                                    kk = 4 * half + k
                                    last = mm3(pe, ps[which][:, :], XTH[:, kk, 0:P], XTL[:, kk, 0:P],
                                               WH[:, s, c], WL[:, s, c], half == 0 and k == 0, half == 1 and k == 3)
                                last.then_inc(S["unit_used"], 1)
                        if which == 0 and has(i, 1, EXPERTS):
                            pe.wait_ge(S["glu_ready"], q)
                            if not (isinstance(i, int) and i == 1) or layer:
                                pe.wait_ge(S["at_lo"], q - 1)
                            for k in range(4):
                                last = pe.transpose(ps[6][:, k * P:(k + 1) * P], AG[:, k * P:(k + 1) * P], ident)
                            last.then_inc(S["at_pe"], 1)
                    if has(i, 0, EXPERTS - 2):
                        gather_transposes(layer, i + 1)
                    if has(i, 1, EXPERTS):
                        pe.wait_ge(S["at_lo"], q)
                        if has(i, 2, 99) or layer:
                            pe.wait_ge(S["y_act"], q - 1)
                            pe.wait_ge(S["y_dve"], q - 1)
                        for half in range(2):
                            j = (0 if isinstance(i, int) and i == EXPERTS else 4) + half
                            s = (s0 + j) % SPLIT
                            pe.wait_ge(S["lo_ready"], u(j) + 1)
                            for k in range(4):
                                c = slice(k * 512, (k + 1) * 512)
                                last = mm3(pe, ps[2 + half][:, :], ATH[:, k, :], ATL[:, k, :],
                                           WH[:, s, c], WL[:, s, c], k == 0, k == 3)
                            last.then_inc(S["unit_used"], 1)
                moe_steps(pe, layer, None, step)
                pe.wait_ge(S["y_act"], EXPERTS * (layer + 1))
                pe.wait_ge(S["y_dve"], EXPERTS * (layer + 1))
                overflow(pe, layer, overflow_pe)

            def overflow_pe(n, v):
                pe.wait_ge(v["gathered"], 16 * n + 16)
                for half in range(2):
                    for k in range(4):
                        last = pe.transpose(ps[4 + half][:, k * P:(k + 1) * P],
                                            XG[:, (4 * half + k) * P:(4 * half + k + 1) * P], ident)
                    last.then_inc(v["x_pe"], 1)
                pe.wait_ge(v["x_copied"], 2 * n + 2)
                for j in range(4):
                    pe.wait_ge(v["weights"], 96 * n + 16 * (j + 1))
                    for k in range(4):
                        last = pe.matmul(ps[j // 2][:, :], XO[:, 4 * (j % 2) + k, :], WOV[:, k * 512:(k + 1) * 512],
                                         start=j % 2 == 0 and k == 0, stop=j % 2 == 1 and k == 3)
                    last.then_inc(v["used"], 1)
                pe.wait_ge(v["glu"], n + 1)
                for k in range(4):
                    last = pe.transpose(ps[6][:, k * P:(k + 1) * P], AG[:, k * P:(k + 1) * P], ident)
                last.then_inc(v["a_pe"], 1)
                pe.wait_ge(v["a_copied"], n + 1)
                for j in range(2):
                    pe.wait_ge(v["weights"], 96 * n + 16 * (5 + j))
                    for k in range(4):
                        last = pe.matmul(ps[2 + j][:, :], AO[:, k, :], WOV[:, k * 512:(k + 1) * 512],
                                         start=k == 0, stop=k == 3)
                    last.then_inc(v["used"], 1)

            def ple(layer, n_xt):
                transposes(n_xt, 4, hn, rows(2 if layer == 0 else 5))
                dense(f"pg{layer}0", PG[layer], 0, n_xt, lambda j: None)
                dense(f"pg{layer}1", PG[layer] + 2, 4, n_xt, xt_free(n_xt))

            for j in range(4):
                wait_freed(pe, "go0", j)
            transposes(2, 4, hn, rows(1))
            for j in range(4):
                wait_freed(pe, "go1", j)
            router(0, 2)
            moe(0)
            ple(0, 3)

            for j in range(4):
                wait_freed(pe, "pg00", j)
            transposes(4, 0, hn, rows(3))
            dense("sv0", SV[0], 4, 4, after("pg01"))
            dense("sv1", SV[1], 0, 4, xt_free(4))
            dense("sv2", SV[2], 4, 4, after("sv0"))
            dense("sv3", SV[3], 0, 4, after("sv1"))
            for c in range(4):
                dense(f"su{c}", SU[c], 4, 4, after("sv2" if c == 0 else f"su{c - 1}"))
                pe.wait_ge(S["ln_done"], 2 * NT)
                for t in range(NT):
                    if c == 0:
                        wait_freed(pe, "sv3", t)
                    else:
                        pe.wait_ge(S["prod_done"], 8 * (c - 1) + 2 * t + 2)
                    for gg in range(2):
                        g = 2 * c + gg
                        last = pe.matmul(ps[t][:, gg * 256:(gg + 1) * 256], WST[:, g, :],
                                         VS[:, t, g * 256:(g + 1) * 256], start=True, stop=True)
                    last.then_inc(S["s_done"], 1)
            for half in range(2):
                n = 5 + half
                if half == 0:
                    for j in range(4):
                        wait_freed(pe, "su3", j)
                    ready = lambda t: pe.wait_ge(S["prod_done"], 16)
                else:
                    for j in range(4):
                        wait_freed(pe, "so00", j)
                    ready = lambda t: pe.wait_ge(S["prod_done"], 32)
                base = 4 if half == 0 else 0
                transposes(n, base, lambda t, k, half=half: VS[:, t, half * D + k * P:half * D + (k + 1) * P], ready)
                dense(f"so{half}0", SO[half][0], 4 - base, n,
                      (lambda j: pe.wait_ge(S["prod_done"], 32)) if half == 0 else after("so01"))
                dense(f"so{half}1", SO[half][1], base, n, xt_free(n))
            for j in range(4):
                wait_freed(pe, "so10", j)
            transposes(7, 4, hn, rows(4))
            for j in range(4):
                wait_freed(pe, "so11", j)
            router(1, 7)
            moe(1)
            ple(1, 8)

        @block.scalar
        def _(act):
            split = Splitter(act, True)
            steps = [0]

            def link(ins):
                steps[0] += 1
                ins.then_inc(S["act_chain"], 1)
                act.wait_ge(S["act_chain"], steps[0])

            def stat(m, t, ready, junk):
                ready(t)
                if m:
                    act.wait_ge(S["rows_ready"], 4 * m)
                link(act.activation(junk, H[:, t, :], ACT.Square, accum_out=square_sum[:, t:t + 1]))
                act.activation(root[:, t:t + 1], square_sum[:, t:t + 1], ACT.Sqrt, bias=EPS, scale=1.0 / D)\
                    .then_inc(S["rms_ready"], 1)

            def high(n, base, t):
                for half in range(2):
                    act.wait_ge(S["xt_pe"], 8 * n + 2 * t + half + 1)
                    src = ps[base + 2 * (t % 2) + half][:, :].rearrange("p (k s) -> p k s", k=4)
                    act.activation(XTH[:, 4 * half:4 * half + 4, t * P:(t + 1) * P], src, ACT.Copy)\
                        .then_inc(S["xt_hi"], 1)

            def norm_phase(n, base, m, ready, junk):
                stat(m, 0, ready, junk)
                stat(m, 1, ready, junk)
                for t in range(NT):
                    high(n, base, t)
                    if t + 2 < NT:
                        stat(m, t + 2, ready, junk)

            def dense_out(name, u0, base, body):
                split.to(u0 + AHEAD)
                split.to(u0 + 1 + AHEAD)
                for j in range(4):
                    wait_tile(act, name, u0 + 1, j)
                    body(j, ps[base + j]).then_inc(S["freed_act"], 1)

            def early(src, dst, k):
                act.activation(dst, src, ACT.Copy).then_inc(S["early_split_hi"], 1)

            act.wait_ge(S["misc_loaded"], MISC)
            early(rwa[:, :, :], WAH[:, :, :], 0)
            early(rwr[:, :, :, :], RWH[:, :, :, :], 1)
            split.to(1)
            junk1 = E1[:, 0:2, :].rearrange("p a s -> p (a s)")
            norm_phase(0, 0, 0, lambda t: act.wait_ge(S["x_loaded"], 16), junk1)

            act.wait_ge(S["a_done"], 1)
            act.activation(aT[:, :], ps[4][:, :], ACT.Copy).then_inc(S["a_copied"], 1)

            def softplus(h):
                act.wait_ge(S["z_done"], h + 1)
                bias = small[:, S_BG + h:S_BG + h + 1]
                act.activation(E1[:, h, :], ps[4 + h][:, :], ACT.Abs, bias=bias).then_inc(S["abs_read"], 1)
                act.wait_ge(S["abs_read"], h + 1)
                link(act.activation(E1[:, h, :], E1[:, h, :], ACT.Exp, scale=-1.0))
                act.activation(E1[:, h, :], E1[:, h, :], ACT.Ln, bias=1.0).then_inc(S["decay_act"], 1)

            def decays(h):
                act.wait_ge(S["bc_ready"], h + 1)
                act.activation(E1[:, h, :], bcum[:, h % 2, :], ACT.Exp, scale=1.0 / TAU)
                act.activation(E2[:, h, :], bcum[:, h % 2, :], ACT.Exp, scale=-1.0 / TAU)
                act.wait_ge(S["dlt_ready"], h + 1)
                act.activation(E3[:, h, :], E3[:, h, :], ACT.Exp, scale=1.0 / TAU).then_inc(S["e_ready"], 1)

            def copy_v(c):
                return lambda j, bank: act.activation(VG[:, j, c * 512:(c + 1) * 512], bank[:, :], ACT.Copy)

            def silu_r(c):
                return lambda j, bank: act.activation(SR[:, j, c * 512:(c + 1) * 512], bank[:, :], ACT.Silu)

            split.to(V0 + 1 + AHEAD)
            for h in range(HEADS):
                softplus(h)
                if h >= 1:
                    decays(h - 1)
                if h == 0:
                    for j in range(4):
                        wait_tile(act, "v0", V0 + 1, j)
                        copy_v(0)(j, ps[j]).then_inc(S["freed_act"], 1)
            decays(HEADS - 1)
            split.to(Q + AHEAD)
            split.to(K + AHEAD)
            dense_out("v1", V1, 0, copy_v(1))
            dense_out("r0", R0, 4, silu_r(0))
            dense_out("r1", R1, 0, silu_r(1))
            act.wait_ge(S["kt_done"], NT)
            KT = E3[:, :, :].rearrange("p h s -> p (h s)").rearrange("p (t f) -> p t f", t=NT)
            for t in range(NT):
                act.activation(KT[:, t, :], ps[4 + t][:, :], ACT.Copy).then_inc(S["kt_copied"], 1)
            for t in range(NT):
                act.wait_ge(S["o_done"], t + 1)
                if t:
                    act.wait_ge(S["o_gated"], t)
                ob = 2 if t % 2 == 0 else 6
                for h in range(HEADS):
                    src = ps[ob + h // 2][:, (h % 2) * HV:(h % 2 + 1) * HV]
                    link(act.activation(o_junk[:, :], src, ACT.Square, accum_out=oss[:, 0, h:h + 1]))
                act.activation(oss[:, 1, :], oss[:, 0, :], ACT.Sqrt, bias=EPS, scale=1.0 / HV).then_inc(S["o_root"], 1)
            for t in range(NT):
                high(1, 0, t)
            split.to(GO0 + 1 + AHEAD)
            split.to(GO1 + 1 + AHEAD)

            def split_p(layer):
                act.wait_ge(S["pt_loaded"], 16 * layer + 16)
                act.activation(pTH[:, :, :], pT[:, :, :], ACT.Copy).then_inc(S["pt_hi"], 1)

            def route(layer):
                split.to(UP[layer] + AHEAD)
                act.wait_ge(S["exp_in"], 2 * layer + 1)
                act.activation(r4[:, 1, :, :], r4[:, 0, :, :], ACT.Exp).then_inc(S["exp_out"], 1)

                def up(c, t):
                    if c == 1 and t == NT - 1:
                        act.wait_ge(S["unit_used"], UP[layer] + 1)
                    else:
                        act.wait_ge(S["up_done"], 7 * layer + 4 * c + t + 1)
                    act.activation(PU[:, t, c * 512:(c + 1) * 512], ps[t][:, :], ACT.Copy)\
                        .then_inc(S["freed_act"], 1)
                for t in range(NT):
                    up(0, t)
                act.wait_ge(S["exp_in"], 2 * layer + 2)
                act.activation(r1t[:, 3, :], r1t[:, 2, :], ACT.Exp).then_inc(S["exp_out"], 1)
                for t in range(NT):
                    up(1, t)

            def moe(layer):
                def step(i, split_to):
                    q = EXPERTS * layer + i
                    jmax = 3 if isinstance(i, int) and i == 0 else 1 if isinstance(i, int) and i == EXPERTS else 5
                    if isinstance(i, int) and i > EXPERTS:
                        jmax = -1
                    last_step = isinstance(i, int) and i == EXPERTS

                    def ahead(*js):
                        for j in js:
                            if j <= jmax:
                                split_to(j)

                    if isinstance(i, int) and i == 0:
                        gather_high(layer, 0)
                    if has(i, 2, EXPERTS + 1):
                        act.wait_ge(S["unit_used"], last_down(layer, i - 2) + 1)
                        if not (isinstance(i, int) and i == 2 and layer == 0):
                            y_free(act, q - 2, i)
                        act.activation(Y[:, 0:512], ps[2][:, :], ACT.Copy).then_inc(S["y_act"], 1)
                    if not last_step:
                        ahead(0, 1)
                    if has(i, 1, EXPERTS):
                        act.wait_ge(S["at_pe"], q)
                        act.activation(ATH[:, :, :], ps[6][:, :].rearrange("p (k s) -> p k s", k=4), ACT.Copy)\
                            .then_inc(S["at_hi"], 1)
                    if has(i, 0, EXPERTS - 1):
                        act.wait_ge(S["unit_used"], unit_of(layer, i, 1) + 1)
                        if has(i, 1, 99) or layer:
                            if not (isinstance(i, int) and i == 0 and layer == 0):
                                act.wait_ge(S["glu_ready"], q)
                        act.activation(SG[:, :], ps[0][:, :], ACT.Silu).then_inc(S["silu_ready"], 1)
                    ahead(*((0, 1) if last_step else (2, 3)))
                    if has(i, 0, EXPERTS - 2):
                        gather_high(layer, i + 1)
                    ahead(4, 5)
                moe_steps(act, layer, split, step)

                def overflow_act(n, v, gate_unit, down_unit):
                    for half in range(2):
                        act.wait_ge(v["x_pe"], 2 * n + half + 1)
                        act.activation(XO[:, 4 * half:4 * half + 4, :],
                                       ps[4 + half][:, :].rearrange("p (k s) -> p k s", k=4), ACT.Copy)\
                            .then_inc(v["x_copied"], 1)

                    def load(j, u):
                        src = weight_stream[u] if isinstance(u, int) else \
                            weight_stream[bass.ds(u, 1)].rearrange("u p f -> p (u f)")
                        if j:
                            act.wait_ge(v["used"], 6 * n + j)
                        act.dma_start(WOV[:, :], src).then_inc(v["weights"], 16)

                    for j in range(4):
                        load(j, gate_unit + j)
                    act.activation(SG[:, :], ps[0][:, :], ACT.Silu).then_inc(v["silu"], 1)
                    act.wait_ge(v["a_pe"], n + 1)
                    act.activation(AO[:, :, :], ps[6][:, :].rearrange("p (k s) -> p k s", k=4), ACT.Copy)\
                        .then_inc(v["a_copied"], 1)
                    for j in range(2):
                        load(4 + j, down_unit + j)
                    act.wait_ge(v["used"], 6 * n + 6)
                    for half in range(2):
                        act.activation(Y[:, half * 512:(half + 1) * 512], ps[2 + half][:, :], ACT.Copy)\
                            .then_inc(v["y"], 1)

                rounds = act.value_load(rounds_i[0:1, 0:1], min_val=1, max_val=ROUNDS)
                with act.If(rounds > 1):
                    with act.Fori(1, rounds) as r:
                        overflow_act((r - 1) * EXPERTS, OV[layer], unit_of(layer, 0, 0), unit_of(layer, 1, 4))
                        with act.Fori(1, EXPERTS - 1) as e:
                            overflow_act((r - 1) * EXPERTS + e, OV[layer],
                                         PER_EXPERT * e + unit_of(layer, 0, 0) - 2,
                                         PER_EXPERT * e + unit_of(layer, 1, 4))
                        overflow_act((r - 1) * EXPERTS + EXPERTS - 1, OV[layer], unit_of(layer, EXPERTS - 1, 0),
                                     unit_of(layer, EXPERTS, 0))

            def gather_high(layer, e):
                q = EXPERTS * layer + e
                for half in range(2):
                    act.wait_ge(S["gx_pe"], 2 * q + half + 1)
                    act.activation(XTH[:, 4 * half:4 * half + 4, 0:P],
                                   ps[4 + half][:, :].rearrange("p (k s) -> p k s", k=4), ACT.Copy)\
                        .then_inc(S["gx_hi"], 1)

            def ple(layer, n, m):
                norm_phase(n, 4, m, lambda t: act.wait_ge(S["combined"], 4 * layer + t + 1), junk3[:, :])
                for c in range(2):
                    def body(j, bank, c=c):
                        if c == 1:
                            act.wait_ge(S["ple_added"], 8 * layer + j + 1)
                        return act.activation(GT[:, j, :], bank[:, :], ACT.Sigmoid)
                    dense_out(f"pg{layer}{c}", PG[layer] + 2 * c, 4 * c, body)

            norm_phase(2, 4, 1, lambda t: wait_freed(act, "go1", t), junk3[:, :])
            split_p(0)
            route(0)
            moe(0)
            ple(0, 3, 2)

            norm_phase(4, 0, 3, lambda t: act.wait_ge(S["ple_added"], 4 + t + 1), junk3[:, :])
            for c in range(4):
                def gelu_v(j, bank, c=c):
                    return act.activation(VS[:, j, c * 512:(c + 1) * 512], bank[:, :], ACT.Gelu_apprx_tanh,
                                          accum_out=vsum[:, j, c:c + 1])
                dense_out(f"sv{c}", SV[c], 4 if c % 2 == 0 else 0, gelu_v)
            split.to(SU[0] + AHEAD)
            for t in range(NT):
                act.wait_ge(S["mean_ready"], t + 1)
                link(act.activation(UT[:, :, :].rearrange("p a n -> p (a n)"), VS[:, t, :], ACT.Square,
                                    bias=vst[:, 1, t:t + 1], accum_out=vst[:, 2, t:t + 1]))
                act.activation(vst[:, 3, t:t + 1], vst[:, 2, t:t + 1], ACT.Sqrt, bias=EPS, scale=1.0 / (2 * D))\
                    .then_inc(S["ln_root"], 1)
            for c in range(4):
                def gelu_u(j, bank, c=c):
                    if c:
                        act.wait_ge(S["prod_done"], 8 * (c - 1) + 2 * j + 2)
                    return act.activation(UT[:, j, :], bank[:, :], ACT.Gelu_apprx_tanh)
                dense_out(f"su{c}", SU[c], 4, gelu_u)
            for half in range(2):
                for t in range(NT):
                    high(5 + half, 4 if half == 0 else 0, t)
                for c in range(2):
                    split.to(SO[half][c] + AHEAD)
                    split.to(SO[half][c] + 1 + AHEAD)
            norm_phase(7, 4, 4, lambda t: wait_freed(act, "so11", t), junk3[:, :])
            split_p(1)
            route(1)
            moe(1)
            ple(1, 8, 5)
            for t in range(NT):
                stat(6, t, lambda t: act.wait_ge(S["ple_added"], 12 + t + 1), junk3[:, :])

        @block.vector
        def _(dve):
            split = Splitter(dve, False)
            steps = [0]

            def link(ins):
                steps[0] += 1
                ins.then_inc(S["dve_chain"], 1)
                dve.wait_ge(S["dve_chain"], steps[0])

            def norm(m, n, t, store, gain_no, out_of=None):
                dve.wait_ge(S["rms_ready"], 4 * m + t + 1)
                link(dve.reciprocal(rstd[:, t:t + 1], root[:, t:t + 1]))
                dve.wait_ge(S["gain_loaded"], 16 * gain_no + 16)
                if n is not None:
                    if t >= 2:
                        dve.wait_ge(S["xt_pe"], 8 * n + 2 * (t - 2) + 2)
                        if store is not None:
                            dve.wait_ge(hn_stored[t % 2], 32 * store + 16)
                    dve.scalar_tensor_tensor(out=HN[:, t % 2, :], in0=H[:, t, :], scalar=rstd[:, t:t + 1],
                                             in1=gain[:, :], op0=ALU.mult, op1=ALU.mult)\
                        .then_inc(S["rows_ready"], 1)
                else:
                    dve.scalar_tensor_tensor(out=H[:, t, :], in0=H[:, t, :], scalar=rstd[:, t:t + 1],
                                             in1=gain[:, :], op0=ALU.mult, op1=ALU.mult)\
                        .then_inc(S["out_ready"], 1)

            def low(n, base, t):
                for half in range(2):
                    dve.wait_ge(S["xt_hi"], 8 * n + 2 * t + half + 1)
                    src = ps[base + 2 * (t % 2) + half][:, :].rearrange("p (k s) -> p k s", k=4)
                    at = (slice(None), slice(4 * half, 4 * half + 4), slice(t * P, (t + 1) * P))
                    dve.tensor_tensor(XTL[at], src, XTH[at], ALU.subtract).then_inc(S["xt_lo"], 1)

            def norm_phase(n, base, m, gain_no, store=None):
                norm(m, n, 0, store, gain_no)
                norm(m, n, 1, store, gain_no)
                for t in range(NT):
                    low(n, base, t)
                    if t + 2 < NT:
                        norm(m, n, t + 2, store, gain_no)

            def add_out(name, u0, base, c):
                split.to(u0 + AHEAD)
                split.to(u0 + 1 + AHEAD)
                for j in range(4):
                    wait_tile(dve, name, u0 + 1, j)
                    at = H[:, j, c * 512:(c + 1) * 512]
                    dve.tensor_tensor(at, ps[base + j][:, :], at, ALU.add).then_inc(S["freed_dve"], 1)

            dve.memset(empty[:, :], BIG).then_inc(S["pool_chain"], 1)
            for k, (low_part, full, high_part) in enumerate((
                    (WAL[:, :, :], rwa[:, :, :], WAH[:, :, :]),
                    (RWL[:, :, :, :], rwr[:, :, :, :], RWH[:, :, :, :]))):
                dve.wait_ge(S["early_split_hi"], k + 1)
                dve.tensor_tensor(low_part, full, high_part, ALU.subtract).then_inc(S["early_split_lo"], 1)
            split.to(1)
            norm_phase(0, 0, 0, 0)

            split.to(V0 + 1 + AHEAD)
            for h in range(HEADS):
                bias = small[:, S_BG + h:S_BG + h + 1]
                dve.wait_ge(S["z_done"], h + 1)
                dve.wait_ge(S["abs_read"], h + 1)
                link(dve.tensor_scalar(E2[:, h, :], ps[4 + h][:, :], bias, 0.0, ALU.add, ALU.min))
                dve.wait_ge(S["decay_act"], h + 1)
                dve.tensor_tensor(E2[:, h, :], E2[:, h, :], E1[:, h, :], ALU.subtract).then_inc(S["z_read"], 1)
                dve.wait_ge(S["z_read"], h + 1)
                if h >= 2:
                    dve.wait_ge(S["e_ready"], h - 1)
                dve.tensor_tensor_scan(bcum[:, h % 2, :], scan_mask[:, :], E2[:, h, :], 0.0, ALU.mult, ALU.add)\
                    .then_inc(S["bc_ready"], 1)
                dve.wait_ge(S["bc_ready"], h + 1)
                b3 = bcum[:, h % 2, :].rearrange("p (n i) -> p n i", i=CHUNK)
                dve.tensor_tensor(E3[:, h, :].rearrange("p (n i) -> p n i", i=CHUNK),
                                  b3[:, :, CHUNK - 1:CHUNK].broadcast_to([P, SEQ // CHUNK, CHUNK]), b3,
                                  ALU.subtract).then_inc(S["dlt_ready"], 1)
            split.to(Q + AHEAD)
            split.to(Q + 1 + AHEAD)
            for h in range(HEADS):
                dve.wait_ge(S["e_ready"], h + 1)
                link(dve.tensor_copy(chunk_decay[:, h, :],
                                     E1[:, h, :].rearrange("p (n i) -> p n i", i=CHUNK)[:, :, CHUNK - 1]))
                wait_tile(dve, "q", Q + 1, h)
                dve.scalar_tensor_tensor(out=E1[:, h, :], in0=ps[h][:, :], scalar=float(P) ** -0.5, in1=E1[:, h, :],
                                         op0=ALU.mult, op1=ALU.mult).then_inc(S["freed_dve"], 1)
            split.to(K + AHEAD)
            split.to(K + 1 + AHEAD)
            for h in range(HEADS):
                wait_tile(dve, "k", K + 1, h)
                dve.tensor_tensor(E2[:, h, :], ps[4 + h][:, :], E2[:, h, :], ALU.mult)
                dve.tensor_tensor(E3[:, h, :], ps[4 + h][:, :], E3[:, h, :], ALU.mult)\
                    .then_inc(S["freed_dve"], 1)
            for u in range(V1, R1 + 2):
                split.to(u + AHEAD)
            dve.wait_ge(S["gain_loaded"], 32)
            for t in range(NT):
                wait_freed(dve, "r1", t)
                dve.tensor_tensor(SR[:, t, :], SR[:, t, :], gain[:, :], ALU.mult).then_inc(S["sr_scaled"], 1)

            def mask(t):
                dve.wait_ge(S["score_done"], t + 1)
                if t >= 2:
                    dve.wait_ge(S["o_done"], t - 1)
                dve.tensor_tensor(AS[:, t % 2, :, :], ps[t % 2][:, :].rearrange("p (h i) -> p h i", h=HEADS),
                                  chunk_mask.unsqueeze(1).broadcast_to([P, HEADS, P]), ALU.mult)\
                    .then_inc(S["mask_done"], 1)

            mask(0)
            for t in range(NT):
                if t + 1 < NT:
                    mask(t + 1)
                for c in range(2):
                    n = 2 * t + c
                    if n == SEQ // CHUNK - 1:
                        break
                    dve.wait_ge(S["kv_done"], n + 1)
                    if n:
                        dve.wait_ge(S["state_ready"], n)
                        dve.wait_ge(S["o_done"], (n - 1) // 2 + 1)
                    for h in range(HEADS):
                        kv = ps[4 + h // 2][:, (h % 2) * HV:(h % 2 + 1) * HV]
                        if n == 0:
                            last = dve.tensor_copy(ST[:, 1, h, :], kv)
                        else:
                            last = dve.scalar_tensor_tensor(
                                out=ST[:, (n + 1) % 2, h, :], in0=ST[:, n % 2, h, :],
                                scalar=chunk_decay[:, h, n:n + 1], in1=kv, op0=ALU.mult, op1=ALU.add)
                    last.then_inc(S["state_ready"], 1)
                dve.wait_ge(S["o_root"], t + 1)
                link(dve.reciprocal(oss[:, 2, :], oss[:, 1, :]))
                dve.wait_ge(S["sr_scaled"], t + 1)
                ob = 2 if t % 2 == 0 else 6
                for h in range(HEADS):
                    at = SR[:, t, h * HV:(h + 1) * HV]
                    last = dve.scalar_tensor_tensor(out=at, in0=ps[ob + h // 2][:, (h % 2) * HV:(h % 2 + 1) * HV],
                                                    scalar=oss[:, 2, h:h + 1], in1=at, op0=ALU.mult, op1=ALU.mult)
                last.then_inc(S["o_gated"], 1)
                dve.wait_ge(S["o_gated"], t + 1)
            for t in range(NT):
                low(1, 0, t)
            add_out("go0", GO0, 4, 0)
            add_out("go1", GO1, 0, 1)

            def split_p(layer):
                dve.wait_ge(S["pt_hi"], layer + 1)
                dve.tensor_tensor(pTL[:, :, :], pT[:, :, :], pTH[:, :, :], ALU.subtract).then_inc(S["pt_lo"], 1)

            def route(layer):
                split.to(UP[layer] + AHEAD)
                L4 = [P, NT, 4]
                dve.wait_ge(S["router_done"], layer + 1)
                bias = small[:, S_RB + 80 * layer:S_RB + 80 * (layer + 1)].rearrange("p (t n) -> p t n", t=NT)
                link(dve.tensor_tensor(lg[:, :, :], ps[6][:, 0:80].rearrange("p (t n) -> p t n", t=NT), bias, ALU.add))
                group = lg[:, :, 0:4]

                def top(values, best, onehot, scratch):
                    link(dve.tensor_reduce(r1t[:, best, :], values, AX.X, ALU.max))
                    link(dve.tensor_tensor(r4[:, onehot, :, :], values,
                                           r1t[:, best, :].unsqueeze(2).broadcast_to(L4), ALU.is_equal))
                    link(dve.tensor_tensor(r4[:, onehot, :, :], r4[:, onehot, :, :], tie, ALU.mult))
                    link(dve.tensor_reduce(r1t[:, scratch, :], r4[:, onehot, :, :], AX.X, ALU.max))
                    link(dve.tensor_tensor(r4[:, onehot, :, :], r4[:, onehot, :, :],
                                           r1t[:, scratch, :].unsqueeze(2).broadcast_to(L4), ALU.is_equal))

                top(group, 0, 2, 1)
                dve.tensor_tensor(r4[:, 0, :, :], group, r1t[:, 0, :].unsqueeze(2).broadcast_to(L4), ALU.subtract)\
                    .then_inc(S["exp_in"], 1)
                L16 = [P, NT, 4, 4]
                v44 = lambda k: r16[:, k, :, :].rearrange("p t (g e) -> p t g e", g=4)
                chosen = r4[:, 2, :, :].unsqueeze(3).broadcast_to(L16)
                link(dve.tensor_tensor(v44(0), lg[:, :, 4:20].rearrange("p t (g e) -> p t g e", g=4), chosen,
                                       ALU.mult))
                link(dve.tensor_reduce(r4[:, 3, :, :], r16[:, 0, :, :].rearrange("p t (g e) -> p t e g", g=4),
                                       AX.X, ALU.add))
                top(r4[:, 3, :, :], 4, 4, 1)
                link(dve.scalar_tensor_tensor(out=r4[:, 5, :, :], in0=r4[:, 4, :, :], scalar=FAR, in1=r4[:, 3, :, :],
                                              op0=ALU.mult, op1=ALU.add))
                top(r4[:, 5, :, :], 5, 6, 1)
                dve.tensor_tensor(r1t[:, 2, :], r1t[:, 5, :], r1t[:, 4, :], ALU.subtract).then_inc(S["exp_in"], 1)
                link(dve.tensor_tensor(v44(1), chosen, r4[:, 4, :, :].unsqueeze(2).broadcast_to(L16), ALU.mult))
                link(dve.tensor_tensor(v44(3), chosen, r4[:, 6, :, :].unsqueeze(2).broadcast_to(L16), ALU.mult))
                dve.tensor_tensor(r16[:, 2, :, :], r16[:, 1, :, :], r16[:, 3, :, :], ALU.add)\
                    .then_inc(S["mask16_ready"], 1)
                dve.wait_ge(S["exp_out"], 2 * layer + 2)
                link(dve.tensor_reduce(r1t[:, 6, :], r4[:, 1, :, :], AX.X, ALU.add))
                link(dve.tensor_scalar(r1t[:, 7, :], r1t[:, 3, :], 1.0, None, ALU.add))
                link(dve.tensor_tensor(r1t[:, 8, :], r1t[:, 6, :], r1t[:, 7, :], ALU.mult))
                link(dve.reciprocal(w_tok[:, 0, :], r1t[:, 8, :]))
                link(dve.tensor_tensor(w_tok[:, 1, :], w_tok[:, 0, :], r1t[:, 3, :], ALU.mult))
                dve.wait_ge(S["rank_done"], layer + 1)
                rank = ps[7][:, 0:64].rearrange("p (t e) -> p t e", t=NT)
                link(dve.tensor_scalar(r16[:, 4, :, :], rank, float(P), None, ALU.is_ge))
                for k in range(2, ROUNDS):
                    link(dve.scalar_tensor_tensor(out=r16[:, 4, :, :], in0=rank, scalar=float(k * P),
                                                  in1=r16[:, 4, :, :], op0=ALU.is_ge, op1=ALU.add))
                link(dve.scalar_tensor_tensor(out=r16[:, 5, :, :], in0=rank, scalar=float(ROUNDS * EXPERTS), in1=eoff,
                                              op0=ALU.mult, op1=ALU.add))
                link(dve.scalar_tensor_tensor(out=r16[:, 5, :, :], in0=r16[:, 4, :, :],
                                              scalar=float(EXPERTS - P * ROUNDS * EXPERTS), in1=r16[:, 5, :, :],
                                              op0=ALU.mult, op1=ALU.add))
                for k, which in enumerate((1, 3)):
                    link(dve.tensor_tensor(r16[:, which, :, :], r16[:, which, :, :], r16[:, 5, :, :], ALU.mult))
                    link(dve.tensor_reduce(pos_f[:, k, :], r16[:, which, :, :], AX.X, ALU.add))
                link(dve.tensor_copy(pos_i[:, :], pos_f[:, :, :].rearrange("p k t -> p (k t)")))
                link(dve.tensor_reduce(cnt[:, 0:1], ps[7][:, 64:80], AX.X, ALU.max))
                link(dve.tensor_scalar(cnt[:, 1:2], cnt[:, 0:1], float(P), 1.0, ALU.is_gt, ALU.add))
                for k in range(2, ROUNDS):
                    link(dve.scalar_tensor_tensor(out=cnt[:, 1:2], in0=cnt[:, 0:1], scalar=float(k * P),
                                                  in1=cnt[:, 1:2], op0=ALU.is_gt, op1=ALU.add))
                dve.tensor_copy(rounds_i[:, :], cnt[:, 1:2]).then_inc(S["routed"], 1)
                dve.wait_ge(S["slots_loaded"], 16 * layer + 16)
                dve.tensor_scalar(slot_tokens[:, :], slot_rows[:, :], 1, None, ALU.logical_shift_right)\
                    .then_inc(S["slots_ready"], 1)

            def gather_low(layer, e):
                q = EXPERTS * layer + e
                for half in range(2):
                    dve.wait_ge(S["gx_hi"], 2 * q + half + 1)
                    at = (slice(None), slice(4 * half, 4 * half + 4), slice(0, P))
                    dve.tensor_tensor(XTL[at], ps[4 + half][:, :].rearrange("p (k s) -> p k s", k=4), XTH[at],
                                      ALU.subtract).then_inc(S["gx_lo"], 1)

            def moe(layer):
                def step(i, split_to):
                    q = EXPERTS * layer + i
                    jmax = 3 if isinstance(i, int) and i == 0 else 1 if isinstance(i, int) and i == EXPERTS else 5
                    if isinstance(i, int) and i > EXPERTS:
                        jmax = -1
                    last_step = isinstance(i, int) and i == EXPERTS

                    def ahead(*js):
                        for j in js:
                            if j <= jmax:
                                split_to(j)

                    if isinstance(i, int) and i == 0:
                        gather_low(layer, 0)
                    if has(i, 2, EXPERTS + 1):
                        dve.wait_ge(S["unit_used"], last_down(layer, i - 2) + 1)
                        if not (isinstance(i, int) and i == 2 and layer == 0):
                            y_free(dve, q - 2, i)
                        dve.tensor_copy(Y[:, 512:D], ps[3][:, :]).then_inc(S["y_dve"], 1)
                    if not last_step:
                        ahead(0, 1)
                    if has(i, 1, EXPERTS):
                        dve.wait_ge(S["at_hi"], q)
                        dve.tensor_tensor(ATL[:, :, :], ps[6][:, :].rearrange("p (k s) -> p k s", k=4),
                                          ATH[:, :, :], ALU.subtract).then_inc(S["at_lo"], 1)
                    ahead(*((0, 1) if last_step else (2, 3)))
                    if has(i, 0, EXPERTS - 1):
                        dve.wait_ge(S["silu_ready"], q + 1)
                        dve.wait_ge(S["unit_used"], unit_of(layer, i, 3) + 1)
                        dve.tensor_tensor(AG[:, :], ps[1][:, :], SG[:, :], ALU.mult).then_inc(S["glu_ready"], 1)
                    if has(i, 0, EXPERTS - 2):
                        gather_low(layer, i + 1)
                    ahead(4, 5)
                moe_steps(dve, layer, split, step)

                def overflow_dve(n, v):
                    dve.wait_ge(v["silu"], n + 1)
                    dve.wait_ge(v["used"], 6 * n + 4)
                    dve.tensor_tensor(AG[:, :], ps[1][:, :], SG[:, :], ALU.mult).then_inc(v["glu"], 1)
                overflow(dve, layer, overflow_dve)

            def combine(layer):
                for t in range(NT):
                    dve.wait_ge(y_loaded[t % 2], 16 * (2 * layer + t // 2 + 1))
                    link(dve.scalar_tensor_tensor(out=H[:, t, :], in0=Y2[:, t % 2, 0:D], scalar=w_tok[:, 0, t:t + 1],
                                                  in1=H[:, t, :], op0=ALU.mult, op1=ALU.add))
                    dve.scalar_tensor_tensor(out=H[:, t, :], in0=Y2[:, t % 2, D:2 * D], scalar=w_tok[:, 1, t:t + 1],
                                             in1=H[:, t, :], op0=ALU.mult, op1=ALU.add).then_inc(S["combined"], 1)

            def ple(layer, n, m, gain_no):
                combine(layer)
                norm_phase(n, 4, m, gain_no)
                for c in range(2):
                    split.to(PG[layer] + 2 * c + AHEAD)
                    split.to(PG[layer] + 2 * c + 1 + AHEAD)
                    for j in range(4):
                        wait_freed(dve, f"pg{layer}{c}", j)
                        at = slice(c * 512, (c + 1) * 512)
                        link(dve.tensor_tensor(GT[:, j, :], GT[:, j, :], PU[:, j, at], ALU.mult))
                        dve.tensor_tensor(H[:, j, at], H[:, j, at], GT[:, j, :], ALU.add).then_inc(S["ple_added"], 1)

            norm_phase(2, 4, 1, 2, store=0)
            split_p(0)
            route(0)
            moe(0)
            ple(0, 3, 2, 3)

            norm_phase(4, 0, 3, 4)
            dve.wait_ge(S["ws_loaded"], 16)
            dve.tensor_tensor(WST[:, :, :], WST[:, :, :], causal.unsqueeze(1).broadcast_to([P, 8, P]), ALU.mult)\
                .then_inc(S["ws_masked"], 1)
            for c in range(4):
                split.to(SV[c] + AHEAD)
                split.to(SV[c] + 1 + AHEAD)
            for t in range(NT):
                wait_freed(dve, "sv3", t)
                link(dve.tensor_reduce(vst[:, 0, t:t + 1], vsum[:, t, :], AX.X, ALU.add))
                dve.tensor_scalar(vst[:, 1, t:t + 1], vst[:, 0, t:t + 1], -1.0 / (2 * D), None, ALU.mult)\
                    .then_inc(S["mean_ready"], 1)
            for t in range(NT):
                dve.wait_ge(S["ln_root"], t + 1)
                link(dve.reciprocal(vst[:, 4, t:t + 1], vst[:, 3, t:t + 1]))
                link(dve.tensor_scalar(VS[:, t, :], VS[:, t, :], vst[:, 1, t:t + 1], vst[:, 4, t:t + 1],
                                       ALU.add, ALU.mult))
            for half in range(2):
                dve.wait_ge(S["ln_loaded"], 32 * half + 32)
                for t in range(NT):
                    at = VS[:, t, half * D:(half + 1) * D]
                    link(dve.tensor_tensor(at, at, lnG[:, :], ALU.mult))
                    dve.tensor_tensor(at, at, lnB[:, :], ALU.add).then_inc(S["ln_done"], 1)
            for c in range(4):
                split.to(SU[c] + AHEAD)
                split.to(SU[c] + 1 + AHEAD)
                for t in range(NT):
                    wait_freed(dve, f"su{c}", t)
                    dve.wait_ge(S["s_done"], 4 * c + t + 1)
                    for gg in range(2):
                        g = 2 * c + gg
                        dve.scalar_tensor_tensor(
                            out=VS[:, t, g * 256:(g + 1) * 256], in0=ps[t][:, gg * 256:(gg + 1) * 256],
                            scalar=small[:, S_BS + g:S_BS + g + 1], in1=UT[:, t, gg * 256:(gg + 1) * 256],
                            op0=ALU.add, op1=ALU.mult).then_inc(S["prod_done"], 1)
            for half in range(2):
                for t in range(NT):
                    low(5 + half, 4 if half == 0 else 0, t)
                for c in range(2):
                    add_out(f"so{half}{c}", SO[half][c], 4 * ((half + c) % 2), c)
            norm_phase(7, 4, 4, 5, store=1)
            split_p(1)
            route(1)
            moe(1)
            ple(1, 8, 5, 6)
            for t in range(NT):
                norm(6, None, t, None, 7)

        @block.gpsimd
        def _(pool):
            copies = [0]

            def load_gain(k, ready):
                ready()
                pool.dma_start(gain[:, :], gains_in[k]).then_inc(S["gain_loaded"], 16)

            def after_rows(m):
                return lambda: pool.wait_ge(S["rows_ready"], 4 * m + 4)

            load_gain(0, lambda: None)
            pool.wait_ge(S["pool_chain"], 1)
            for layer in range(2):
                pool.dma_start(list_dram[layer].rearrange("(p f) o -> p (f o)", p=P), empty[:, :])\
                    .then_inc(S["list_cleared"], 16)
            load_gain(1, after_rows(0))
            load_gain(2, lambda: pool.wait_ge(S["sr_scaled"], NT))
            pool.wait_ge(S["o_gated"], NT)
            pool.dma_start(pT[:, :, :], pt_in[0]).then_inc(S["pt_loaded"], 16)

            def store_rows(layer, m):
                for t in range(NT):
                    pool.wait_ge(S["rows_ready"], 4 * m + t + 1)
                    pool.dma_start(hn_dram[layer][t * P:(t + 1) * P, :], HN[:, t % 2, :]).then_inc(hn_stored[t % 2], 16)
                    if t == 0:
                        pool.memset(XG[:, :], 0.0).then_inc(S["pool_chain"], 1)

            def gather(layer, e):
                q = EXPERTS * layer + e
                first = isinstance(e, int) and e == 0
                if not first:
                    pool.wait_ge(S["gx_pe"], 2 * q)
                if not (first and layer == 0):
                    pool.wait_ge(S["gathered"], 16 * q)
                col(slot_tokens, e, gather_col)
                pool.indirect_dma_start(out=XG[:, :], out_offset=None, in_=hn_dram[layer],
                                        in_offset=bass.IndirectOffsetOnAxis(ap=gather_col[:, :], axis=0),
                                        bounds_check=SEQ - 1, oob_is_err=False).then_inc(S["gathered"], 16)

            def scatter(layer, e):
                q = EXPERTS * layer + e
                pool.wait_ge(S["y_act"], q + 1)
                pool.wait_ge(S["y_dve"], q + 1)
                if not (isinstance(e, int) and e == 0 and layer == 0):
                    pool.wait_ge(S["scattered"], 16 * q)
                col(slot_rows, e, scatter_col)
                pool.indirect_dma_start(out=y_dram[layer], out_offset=bass.IndirectOffsetOnAxis(ap=scatter_col[:, :], axis=0),
                                        in_=Y[:, :], in_offset=None,
                                        bounds_check=2 * SEQ - 1, oob_is_err=False).then_inc(S["scattered"], 16)

            def col(table, c, to):
                copies[0] += 1
                pool.tensor_copy(to[:, :], table[:, c:c + 1]).then_inc(S["col_copied"], 1)
                pool.wait_ge(S["col_copied"], copies[0])

            def moe(layer, m):
                pool.wait_ge(S["routed"], layer + 1)
                pool.wait_ge(S["list_cleared"], 32)
                for k in range(2):
                    for t in range(NT):
                        pool.indirect_dma_start(
                            out=list_dram[layer],
                            out_offset=bass.IndirectOffsetOnAxis(ap=pos_i[:, k * NT + t:k * NT + t + 1], axis=0),
                            in_=ids[:, 2 * t + k:2 * t + k + 1], in_offset=None,
                            bounds_check=SLOTS - 1, oob_is_err=False).then_inc(S["slots_written"], 16)
                pool.wait_ge(S["slots_written"], 16 * 8 * (layer + 1))
                pool.dma_start(slot_rows[:, :], list_dram[layer].rearrange("(p f) o -> p (f o)", p=P))\
                    .then_inc(S["slots_loaded"], 16)
                for b in range(2):
                    pool.wait_ge(hn_stored[b], 32 * layer + 32)
                pool.wait_ge(S["pool_chain"], layer + 2)
                pool.wait_ge(S["slots_ready"], layer + 1)
                for e in range(4):
                    gather(layer, e)
                for i in range(2, EXPERTS + 2):
                    scatter(layer, i - 2)
                    if i + 2 < EXPERTS:
                        gather(layer, i + 2)
                pool.wait_ge(S["scattered"], 16 * EXPERTS * (layer + 1))
                v = OV[layer]
                rounds = pool.value_load(rounds_i[0:1, 0:1], min_val=1, max_val=ROUNDS)
                for r in range(1, ROUNDS):
                    with pool.If(rounds > r):
                        for e in range(EXPERTS):
                            n = (r - 1) * EXPERTS + e
                            c = r * EXPERTS + e
                            pool.tensor_copy(gather_col[:, :], slot_tokens[:, c:c + 1]).then_inc(v["col"], 1)
                            pool.wait_ge(v["col"], 2 * n + 1)
                            pool.indirect_dma_start(
                                out=XG[:, :], out_offset=None, in_=hn_dram[layer],
                                in_offset=bass.IndirectOffsetOnAxis(ap=gather_col[:, :], axis=0),
                                bounds_check=SEQ - 1, oob_is_err=False).then_inc(v["gathered"], 16)
                            pool.tensor_copy(scatter_col[:, :], slot_rows[:, c:c + 1]).then_inc(v["col"], 1)
                            pool.wait_ge(v["col"], 2 * n + 2)
                            pool.wait_ge(v["y"], 2 * n + 2)
                            pool.indirect_dma_start(
                                out=y_dram[layer],
                                out_offset=bass.IndirectOffsetOnAxis(ap=scatter_col[:, :], axis=0),
                                in_=Y[:, :], in_offset=None,
                                bounds_check=2 * SEQ - 1, oob_is_err=False).then_inc(v["scattered"], 16)
                            pool.wait_ge(v["scattered"], 16 * n + 16)
                for t in range(NT):
                    if t >= 2:
                        pool.wait_ge(S["combined"], 4 * layer + t - 1)
                    pool.dma_start(Y2[:, t % 2, :],
                                   y_dram[layer][2 * t * P:2 * (t + 1) * P, :].rearrange("(p k) d -> p (k d)", p=P))\
                        .then_inc(y_loaded[t % 2], 16)

            store_rows(0, 1)
            load_gain(3, after_rows(1))
            moe(0, 1)
            load_gain(4, after_rows(2))
            pool.wait_ge(S["ple_added"], 8)
            pool.dma_start(WST[:, :, :], ws_in).then_inc(S["ws_loaded"], 16)
            for half in range(2):
                if half:
                    pool.wait_ge(S["ln_done"], NT)
                pool.dma_start(lnG[:, :], ln_in[2 * half]).then_inc(S["ln_loaded"], 16)
                pool.dma_start(lnB[:, :], ln_in[2 * half + 1]).then_inc(S["ln_loaded"], 16)
                if half == 0:
                    load_gain(5, after_rows(3))
            pool.wait_ge(S["xt_pe"], 8 * 7)
            pool.dma_start(pT[:, :, :], pt_in[1]).then_inc(S["pt_loaded"], 16)
            store_rows(1, 4)
            load_gain(6, after_rows(4))
            moe(1, 4)
            load_gain(7, after_rows(5))


def _lay_out(a):
    import numpy as np
    f = {k: np.asarray(v) for k, v in a.items()}
    stream = np.empty((UNITS, P, UNIT), np.float32)
    at = [0]

    def put(w):
        stream[at[0]] = w.reshape(4, P, 512).transpose(1, 0, 2).reshape(P, UNIT)
        at[0] += 1

    def block(w, c):
        for half in range(w.shape[0] // 512):
            put(w[half * 512:(half + 1) * 512, c:c + 512])

    def moe(layer):
        stream[at[0]] = f["ple_w_up"][layer].reshape(2, P, D).transpose(1, 0, 2).reshape(P, UNIT)
        at[0] += 1
        for i in range(EXPERTS + 1):
            if i < EXPERTS:
                block(f["moe_w_gate"][layer, i], 0)
                block(f["moe_w_up"][layer, i], 0)
            if i:
                for c in (0, 512):
                    block(f["moe_w_down"][layer, i - 1], c)
        for c in (0, 512):
            block(f["ple_w_gate"][layer], c)

    w = f["gla_w_in"][0]
    for c in (1024, 0, 512, 1536, 2048, 2560):
        block(w, c)
    for c in (0, 512):
        block(f["gla_w_out"][0], c)
    moe(0)
    w = f["sgu_w_in"][0]
    for c in range(2048, 4096, 512):
        block(w, c)
    for c in range(0, 2048, 512):
        block(w, c)
    for half in range(2):
        for c in (0, 512):
            block(f["sgu_w_out"][0][half * D:(half + 1) * D], c)
    moe(1)
    assert at[0] == UNITS

    def rep(v):
        return np.broadcast_to(v, (P,) + v.shape)

    con = np.zeros((P, C_END), np.float32)
    i, j = np.arange(P)[:, None], np.arange(P)[None, :]
    con[:, C_ID:C_ID + P] = i == j
    con[:, C_ONE:C_ONE + P] = 1
    con[:, C_BEFORE:C_BEFORE + P] = i < j
    con[:, C_CHUNK:C_CHUNK + P] = (i <= j) & (i // CHUNK == j // CHUNK)
    con[:, C_CAUSAL:C_CAUSAL + P] = i <= j
    con[:, C_TIE:C_TIE + 16] = np.tile([4, 3, 2, 1], NT)
    con[:, C_EOFF:C_EOFF + 64] = np.tile(np.arange(16), NT)
    scan = np.tile((np.arange(SEQ) % CHUNK != 0).astype(np.float32), (P, 1))
    ids = np.zeros((P, 2 * NT), np.int32)
    for t in range(NT):
        for k in range(2):
            ids[:, 2 * t + k] = 2 * (t * P + np.arange(P)) + k
    small = np.zeros((P, S_END), np.float32)
    small[:, S_BG:S_BG + 4] = f["gla_b_gate"][0].reshape(4, P).T
    small[:, S_BS:S_BS + 8] = f["sgu_b_s"][0].T
    router = np.empty((P, 2, KD, 20), np.float32)
    for layer in range(2):
        for t in range(NT):
            c = S_RB + 80 * layer + 20 * t
            small[:, c:c + 4] = f["moe_b_route_group"][layer]
            small[:, c + 4:c + 20] = f["moe_b_route_expert"][layer].reshape(16)
        router[:, layer, :, 0:4] = f["moe_w_route_group"][layer].reshape(KD, P, 4).transpose(1, 0, 2)
        router[:, layer, :, 4:20] = f["moe_w_route_expert"][layer].reshape(KD, P, 16).transpose(1, 0, 2)
    wa = np.zeros((P, KD, P), np.float32)
    wa[:, :, 0:16] = f["gla_w_in"][0][:, 3072:3088].reshape(KD, P, 16).transpose(1, 0, 2)
    wgu = np.zeros((P, 512), np.float32)
    wgu[0:16] = f["gla_w_gate_up"][0]
    gains = np.stack([rep(v) for v in (
        f["norm_mix_g"][0], f["gla_g_head"][0], f["norm_ffn_g"][0], f["norm_ple_g"][0],
        f["norm_mix_g"][1], f["norm_ffn_g"][1], f["norm_ple_g"][1], f["final_norm_g"])])
    ln = np.stack([rep(v) for half in range(2) for v in (
        f["sgu_ln_g"][0][half * D:(half + 1) * D], f["sgu_ln_b"][0][half * D:(half + 1) * D])])
    ws = f["sgu_w_s"][0].transpose(2, 0, 1)
    pt = np.stack([f["p"][i, 0].T.reshape(2, P, SEQ).transpose(1, 0, 2) for i in range(2)])
    x = f["x"][0].reshape(NT, P, D).transpose(1, 0, 2)
    return {"weight_stream": stream, "x": x, "constants": con, "ids": ids, "scan": scan, "small": small,
            "gains": gains, "ln": ln, "router": router, "wa": wa, "wgu": wgu, "ws": ws, "pt": pt}


def kernel(**inputs):
    import numpy as _np
    import concourse.bacc as _bacc
    from concourse.bass_utils import run_bass_kernel_spmd as _run

    nc = _bacc.Bacc("TRN2", target_bir_lowering=False, num_devices=1)
    arrays = {f"in_{k}": _np.ascontiguousarray(v) for k, v in _lay_out(inputs).items()}
    args = [nc.dram_tensor(k, v.shape, mybir.dt.from_np(v.dtype), kind="ExternalInput").ap()
            for k, v in arrays.items()]
    out = nc.dram_tensor("out", (NT, P, D), F32, kind="ExternalOutput").ap()
    hn = [nc.dram_tensor(f"hn{i}", (SEQ, D), F32).ap() for i in range(2)]
    y = [nc.dram_tensor(f"y{i}", (2 * SEQ, D), F32).ap() for i in range(2)]
    slots = [nc.dram_tensor(f"slots{i}", (SLOTS, 1), I32).ap() for i in range(2)]
    ins = dict(zip(arrays, args))
    build(nc, ins["in_weight_stream"], ins["in_x"], ins["in_constants"], ins["in_ids"], ins["in_scan"],
          ins["in_small"], ins["in_gains"], ins["in_ln"], ins["in_router"], ins["in_wa"], ins["in_wgu"],
          ins["in_ws"], ins["in_pt"], out, hn, y, slots)
    r = _run(nc, [arrays], core_ids=[0])
    return r.results[0]["out"].reshape(1, SEQ, D)
```

```python
from contextlib import ExitStack

import concourse.bass as bass
from concourse import mybir

F32 = mybir.dt.float32
F32R = mybir.dt.float32r
I32 = mybir.dt.int32
ACT = mybir.ActivationFunctionType
ALU = mybir.AluOpType
AX = mybir.AxisListType

P = 128
D = 1024
SEQ = 512
NT = SEQ // P
KD = D // P
UNIT = 2048
RAW = 3
SPLIT = 3
AHEAD = SPLIT - 1
HEADS = 4
HV = D // HEADS
CHUNK = 64
TAU = 16.0
EXPERTS = 16
PER_EXPERT = 6
EPS = 1e-6
BIG = 1 << 20
ROUNDS = SEQ // P
EXTRA = 2 * SEQ // P - 1
FAR = -3.0e38

V0, Q, K, V1, R0, R1, GO0, GO1 = range(0, 16, 2)
UP = [16, 141]
MOE = [17, 142]
PG = [113, 238]
SV = [117 + 2 * c for c in range(4)]
SU = [125 + 2 * c for c in range(4)]
SO = [[133, 135], [137, 139]]
UNITS = 242
MISC = 16 * 5

C_ID, C_ONE, C_BEFORE, C_CHUNK, C_CAUSAL, C_TIE, C_EOFF = 0, 128, 256, 384, 512, 640, 656
C_NUM = C_EOFF + 64
C_TAB = C_NUM + EXTRA + 1
C_IOTA = C_TAB + 3 * ROUNDS * EXPERTS
C_ROW = C_IOTA + P
C_END = C_ROW + 2 * NT
S_BG, S_BS, S_RB = 0, 4, 12
S_END = 12 + 160


def unit_of(layer, i, j):
    return MOE[layer] + (j if isinstance(i, int) and i == 0 else PER_EXPERT * i - 2 + j)


def build(nc, weight_stream, x_in, consts_in, scan_in, small_in, gains_in, ln_in, router_in, wa_in, wgu_in, ws_in,
          pt_in, out, hn_dram, y_dram):
    stack = ExitStack()
    with stack:
        def sb(name, shape, dt=F32, on=None):
            return (on or stack).enter_context(nc.sbuf_tensor(name, shape, dt))

        def sem(name):
            return stack.enter_context(nc.semaphore(name))

        raw = sb("raw", [P, RAW, UNIT])
        WH = sb("WH", [P, SPLIT, UNIT], F32R)
        WL = sb("WL", [P, SPLIT, UNIT], F32R)
        XTH = sb("XTH", [P, KD, SEQ], F32R)
        XTL = sb("XTL", [P, KD, SEQ], F32R)
        H = sb("H", [P, NT, D])
        HN = sb("HN", [P, 2, D])
        gain = sb("gain", [P, D])
        con = sb("con", [P, C_END])
        small = sb("small", [P, S_END])
        square_sum = sb("square_sum", [P, NT])
        root = sb("root", [P, NT])
        rstd = sb("rstd", [P, NT])
        w_tok = sb("w_tok", [P, 2, NT])
        slot_rows = sb("slot_rows", [P, ROUNDS * EXPERTS], I32)
        slot_tokens = sb("slot_tokens", [P, ROUNDS * EXPERTS], I32)
        gather_col = sb("gather_col", [P, 1], I32)
        scatter_col = sb("scatter_col", [P, 1], I32)
        extra_i = sb("extra_i", [P, 4, EXTRA + 1], I32)

        ident = con[:, C_ID:C_ID + P]
        ones = con[:, C_ONE:C_ONE + P]
        before = con[:, C_BEFORE:C_BEFORE + P]
        chunk_mask = con[:, C_CHUNK:C_CHUNK + P]
        causal = con[:, C_CAUSAL:C_CAUSAL + P]
        tie = con[:, C_TIE:C_TIE + 16].rearrange("p (t e) -> p t e", t=NT)
        eoff = con[:, C_EOFF:C_EOFF + 64].rearrange("p (t e) -> p t e", t=NT)

        iota = con[:, C_IOTA:C_IOTA + P]
        row_number = con[:, C_ROW:C_ROW + 2 * NT]
        numbers = con[:, C_NUM:C_NUM + EXTRA]
        tables = con[:, C_TAB:C_IOTA].rearrange("p (k n) -> p k n", k=3)

        with ExitStack() as r1:
            E1 = sb("E1", [P, HEADS, SEQ], on=r1)
            E2 = sb("E2", [P, HEADS, SEQ], on=r1)
            E3 = sb("E3", [P, HEADS, SEQ], on=r1)
            VG = sb("VG", [P, NT, D], on=r1)
            SR = sb("SR", [P, NT, D], on=r1)
            bcum = sb("bcum", [P, 2, SEQ], on=r1)
            chunk_decay = sb("chunk_decay", [P, HEADS, SEQ // CHUNK], on=r1)
            oss = sb("oss", [P, 3, HEADS], on=r1)
            o_junk = sb("o_junk", [P, HV], on=r1)
        with ExitStack() as r1b:
            sb("skip_E", [P, 3, HEADS * SEQ], on=r1b)
            WAH = sb("WAH", [P, KD, P], F32R, on=r1b)
            WAL = sb("WAL", [P, KD, P], F32R, on=r1b)
            sb("skip_SR", [P, 2 * D], on=r1b)
            WGU = sb("WGU", [P, 4 * P], on=r1b)
            aT = sb("aT", [P, SEQ], on=r1b)
            rwa = sb("rwa", [P, KD, P], on=r1b)
            scan_mask = sb("scan_mask", [P, SEQ], on=r1b)
        with ExitStack() as r2:
            VS = sb("VS", [P, NT, 2 * D], on=r2)
            UT = sb("UT", [P, NT, 512], on=r2)
            WST = sb("WST", [P, 8, P], on=r2)
            lnG = sb("lnG", [P, D], on=r2)
            lnB = sb("lnB", [P, D], on=r2)
            vsum = sb("vsum", [P, NT, 4], on=r2)
            vst = sb("vst", [P, 5, NT], on=r2)
        with ExitStack() as r3:
            PU = sb("PU", [P, NT, D], on=r3)
            junk3 = sb("junk3", [P, D], on=r3)
            pT = sb("pT", [P, 2, SEQ], on=r3)
            pTH = sb("pTH", [P, 2, SEQ], F32R, on=r3)
            pTL = sb("pTL", [P, 2, SEQ], F32R, on=r3)
            with ExitStack() as r3e:
                XG = sb("XG", [P, D], on=r3e)
                SG = sb("SG", [P, 512], on=r3e)
                AG = sb("AG", [P, 512], on=r3e)
                ATH = sb("ATH", [P, 4, P], F32R, on=r3e)
                ATL = sb("ATL", [P, 4, P], F32R, on=r3e)
                Y = sb("Y", [P, D], on=r3e)
            Y2 = sb("Y2", [P, 2, 2 * D], on=r3)
            lg = sb("lg", [P, NT, 20], on=r3)
            r4 = sb("r4", [P, 12, NT, 4], on=r3)
            r16 = sb("r16", [P, 6, NT, 16], on=r3)
            r1t = sb("r1t", [P, 12, NT], on=r3)
            place = sb("place", [P, 5, 2, NT], on=r3)
            extra_f = sb("extra_f", [P, 4, EXTRA + 1], on=r3)
        with ExitStack() as r3w:
            sb("skip_PU_p", [P, 2, NT * D], on=r3w)
            RWH = sb("RWH", [P, KD, P], F32R, on=r3w)
            rw = sb("rw", [P, KD, P], on=r3w)
            sb("skip_AT", [P, 2 * 512], on=r3w)
            RWL = sb("RWL", [P, KD, P], F32R, on=r3w)
        XO = HN[:, 0, :].rearrange("p (k s) -> p k s", k=KD)
        AO = HN[:, 1, 0:512].rearrange("p (k s) -> p k s", k=4)
        with ExitStack() as r3o:
            sb("skip_PU", [P, NT * D], on=r3o)
            WOV = sb("WOV", [P, 2, UNIT], on=r3o)
        slot_marks = junk3[:, :].rearrange("p (a n) -> p a n", a=2 * NT)
        column_rows = AG[:, :].rearrange("p (a n) -> p a n", a=2 * NT)
        GT = Y2[:, 0:1, :].rearrange("p a (j n) -> p (a j) n", j=NT)
        AS = bcum[:, :, :].rearrange("p b (h i) -> p b h i", h=HEADS)
        ST = HN[:, :, :].rearrange("p b (h v) -> p b h v", h=HEADS)

        ps = [stack.enter_context(nc.psum_tensor(f"bank{i}", [P, 512], F32)) for i in range(8)]

        raw_loaded = [sem(f"raw_loaded{i}") for i in range(RAW)]
        S = {n: sem(n) for n in (
            "hi_ready lo_ready unit_used x_loaded misc_loaded gain_loaded ln_loaded pt_loaded rw_loaded rw_hi rw_lo "
            "rows_ready rms_ready xt_pe xt_hi xt_lo tile_done freed_act freed_dve early_split_hi early_split_lo "
            "a_done a_copied z_done z_read abs_read decay_act bc_ready dlt_ready e_ready kt_done kt_copied sr_scaled "
            "score_done mask_done kv_done state_ready o_done o_root o_gated act_chain dve_chain up_done "
            "router_done exp_in exp_out logits_formed logits_copied xg_cleared mask16_ready rank_done marks_ready slots_formed extra_ready slots_ready "
            "pt_hi pt_lo at_pe at_hi at_lo gx_pe gx_hi gx_lo silu_ready glu_ready y_act y_dve gathered scattered "
            "col_copied combined ple_added ln_root ln_done mean_ready s_done prod_done ws_loaded ws_masked "
            "out_ready out_stored").split()}

        hn_stored = [sem(f"hn_stored{b}") for b in range(2)]
        y_loaded = [sem(f"y_loaded{b}") for b in range(2)]
        OV = [{n: sem(f"ov{layer}_{n}") for n in (
            "gathered scattered weights0 weights1 used x_pe x_copied silu glu a_pe a_copied y col".split())} for layer in range(2)]

        act_blocks = ["v0", "v1", "r0", "r1", "up00", "up01", "pg00", "pg01", "sv0", "sv1", "sv2", "sv3",
                      "su0", "su1", "su2", "su3", "up10", "up11", "pg10", "pg11"]
        dve_blocks = ["q", "k", "go0", "go1", "so00", "so01", "so10", "so11"]

        def wait_freed(eng, block, j):
            if block in act_blocks:
                eng.wait_ge(S["freed_act"], 4 * act_blocks.index(block) + j + 1)
            else:
                eng.wait_ge(S["freed_dve"], 4 * dve_blocks.index(block) + j + 1)

        dense_order = ["v0", "q", "k", "v1", "r0", "r1", "go0", "go1", "pg00", "pg01", "sv0", "sv1", "sv2", "sv3",
                       "su0", "su1", "su2", "su3", "so00", "so01", "so10", "so11", "pg10", "pg11"]

        def wait_tile(eng, block, last_unit, j):
            if j < 3:
                eng.wait_ge(S["tile_done"], 3 * dense_order.index(block) + j + 1)
            else:
                eng.wait_ge(S["unit_used"], last_unit + 1)

        def mm3(pe, dst, ah, al, bh, bl, start, stop):
            pe.matmul(dst, ah, bh, start=start, stop=False)
            pe.matmul(dst, ah, bl, start=False, stop=False)
            return pe.matmul(dst, al, bh, start=False, stop=stop)

        block = stack.enter_context(nc.Block())

        @block.sync
        def _(sp):
            sp.dma_start(H[:, :, :], x_in).then_inc(S["x_loaded"], 16)
            sp.dma_start(con[:, :], consts_in).then_inc(S["misc_loaded"], 16)
            sp.dma_start(small[:, :], small_in).then_inc(S["misc_loaded"], 16)
            sp.dma_start(rwa[:, :, :], wa_in).then_inc(S["misc_loaded"], 16)
            sp.dma_start(scan_mask[:, :], scan_in).then_inc(S["misc_loaded"], 16)
            sp.dma_start(WGU[:, :], wgu_in).then_inc(S["misc_loaded"], 16)
            for u in range(RAW):
                sp.dma_start(raw[:, u, :], weight_stream[u]).then_inc(raw_loaded[u], 16)
            turns = UNITS // RAW
            with sp.Fori(1, turns) as n:
                for s in range(RAW):
                    src = weight_stream[bass.ds(n * RAW + s, 1)].rearrange("u p f -> p (u f)")
                    sp.wait_ge(S["lo_ready"], n * RAW + s - RAW + 1)
                    sp.dma_start(raw[:, s, :], src).then_inc(raw_loaded[s], 16)
            for u in range(turns * RAW, UNITS):
                sp.wait_ge(S["lo_ready"], u - RAW + 1)
                sp.dma_start(raw[:, u % RAW, :], weight_stream[u]).then_inc(raw_loaded[u % RAW], 16)
            for t in range(NT):
                sp.wait_ge(S["out_ready"], t + 1)
                sp.dma_start(out[t], H[:, t, :]).then_inc(S["out_stored"], 16)
            sp.wait_ge(S["out_stored"], 16 * NT)

        class Splitter:

            def __init__(self, eng, high):
                self.eng, self.high, self.next = eng, high, 0

            def one(self, u, slot_of):
                rs, ss = slot_of % RAW, slot_of % SPLIT
                if self.high:
                    self.eng.wait_ge(raw_loaded[rs], (u - rs) // RAW * 16 + 16 if isinstance(u, int) else self.turn(u, slot_of))
                    if not isinstance(u, int) or u >= SPLIT:
                        self.eng.wait_ge(S["unit_used"], u - SPLIT + 1)
                    self.eng.activation(WH[:, ss, :], raw[:, rs, :], ACT.Copy).then_inc(S["hi_ready"], 1)
                else:
                    self.eng.wait_ge(S["hi_ready"], u + 1)
                    self.eng.tensor_tensor(WL[:, ss, :], raw[:, rs, :], WH[:, ss, :], ALU.subtract)\
                        .then_inc(S["lo_ready"], 1)

            def turn(self, u, slot_of):
                return (PER_EXPERT // RAW * self.i + slot_of // RAW) * 16 + 16

            def to(self, u_last):
                while self.next <= min(u_last, UNITS - 1):
                    self.one(self.next, self.next)
                    self.next += 1

            def to_in_loop(self, layer, i, j_last):
                self.i = i
                while self.next <= j_last + AHEAD:
                    at0 = MOE[layer] - 2 + self.next
                    self.one(PER_EXPERT * i + at0, at0)
                    self.next += 1

        LOOP = (3, 14)

        def moe_steps(eng, layer, split, step):
            for i in range(LOOP[0]):
                step(i, (lambda j, i=i: split.to(unit_of(layer, i, j) + AHEAD)) if split else None)
            if split:
                split.to(unit_of(layer, LOOP[0], -1) + AHEAD)
                assert split.next == unit_of(layer, LOOP[0], 0) + AHEAD
                split.next = AHEAD
            with eng.Fori(*LOOP) as i:
                step(i, (lambda j: split.to_in_loop(layer, i, j)) if split else None)
                if split:
                    split.to_in_loop(layer, i, 5)
            if split:
                split.next = unit_of(layer, LOOP[1], 0) + AHEAD
            for i in range(LOOP[1], EXPERTS + 2):
                step(i, (lambda j, i=i: split.to(unit_of(layer, i, j) + AHEAD)) if split else None)

        def last_down(layer, e):
            return unit_of(layer, e + 1, 1 if isinstance(e, int) and e == EXPERTS - 1 else 5)

        def y_free(eng, q, i):
            eng.wait_ge(S["scattered"], 16 * q)

        def has(i, lo, hi):
            return not isinstance(i, int) or lo <= i <= hi

        def overflow(eng, layer, body):
            eng.wait_ge(S["extra_ready"], layer + 1)
            count = eng.value_load(extra_i[0:1, 0, 0:1], min_val=0, max_val=EXTRA)
            with eng.If(count > 0):
                with eng.Fori(0, count) as n:
                    body(n, OV[layer])

        @block.tensor
        def _(pe):
            def transposes(n, base, source, ready):
                for t in range(NT):
                    ready(t)
                    for half in range(2):
                        bank = ps[base + 2 * (t % 2) + half]
                        if t >= 2:
                            pe.wait_ge(S["xt_lo"], 8 * n + 2 * (t - 2) + half + 1)
                        for q in range(4):
                            last = pe.transpose(bank[:, q * P:(q + 1) * P], source(t, 4 * half + q), ident)
                        last.then_inc(S["xt_pe"], 1)

            def rows(n):
                return lambda t: pe.wait_ge(S["rows_ready"], 4 * n + t + 1)

            def hn(t, k):
                return HN[:, t % 2, k * P:(k + 1) * P]

            def dense(name, u0, base, n_xt, free, feature_major=False):
                for half in range(2):
                    u = u0 + half
                    s = u % SPLIT
                    pe.wait_ge(S["lo_ready"], u + 1)
                    if feature_major and half == 0:
                        pe.wait_ge(S["xt_lo"], 8 * n_xt + 8)
                    for j in range(4):
                        if half == 0:
                            free(j)
                            if not feature_major:
                                pe.wait_ge(S["xt_lo"], 8 * n_xt + 2 * j + 2)
                        for k in range(4):
                            kk = 4 * half + k
                            start, stop = half == 0 and k == 0, half == 1 and k == 3
                            if feature_major:
                                c = slice(k * 512 + j * P, k * 512 + (j + 1) * P)
                                last = mm3(pe, ps[base + j][:, :], WH[:, s, c], WL[:, s, c],
                                           XTH[:, kk, :], XTL[:, kk, :], start, stop)
                            else:
                                c, r = slice(k * 512, (k + 1) * 512), slice(j * P, (j + 1) * P)
                                last = mm3(pe, ps[base + j][:, :], XTH[:, kk, r], XTL[:, kk, r],
                                           WH[:, s, c], WL[:, s, c], start, stop)
                        if j == 3:
                            last.then_inc(S["unit_used"], 1)
                        elif half == 1:
                            last.then_inc(S["tile_done"], 1)

            def xt_free(n):
                return lambda j: pe.wait_ge(S["xt_lo"], 8 * n + 4 + 2 * (j // 2) + j % 2 + 1)

            def after(name):
                return lambda j: wait_freed(pe, name, j)

            pe.wait_ge(S["misc_loaded"], MISC)
            transposes(0, 0, hn, rows(0))
            pe.wait_ge(S["xt_lo"], 8)
            pe.wait_ge(S["early_split_lo"], 1)
            for k in range(KD):
                last = mm3(pe, ps[4][:, :], WAH[:, k, :], WAL[:, k, :], XTH[:, k, :], XTL[:, k, :],
                           k == 0, k == KD - 1)
            last.then_inc(S["a_done"], 1)
            dense("v0", V0, 0, 0, xt_free(0))
            pe.wait_ge(S["a_copied"], 1)
            for h in range(HEADS):
                pe.matmul(ps[4 + h][:, :], WGU[:, h * P:(h + 1) * P], aT[:, :], start=True, stop=True)\
                    .then_inc(S["z_done"], 1)
            dense("q", Q, 0, 0, after("v0"), True)
            pe.wait_ge(S["z_read"], HEADS)
            dense("k", K, 4, 0, lambda j: None, True)
            dense("v1", V1, 0, 0, after("q"))
            dense("r0", R0, 4, 0, after("k"))
            dense("r1", R1, 0, 0, after("v1"))

            wait_freed(pe, "k", HEADS - 1)
            for t in range(NT):
                wait_freed(pe, "r0", t)
                for h in range(HEADS):
                    last = pe.transpose(ps[4 + t][:, h * P:(h + 1) * P], E3[:, h, t * P:(t + 1) * P], ident)
                last.then_inc(S["kt_done"], 1)
            KT = E3[:, :, :].rearrange("p h s -> p (h s)").rearrange("p (t h k) -> p t h k", t=NT, h=HEADS)
            for j in range(4):
                wait_freed(pe, "r1", j)

            def scores(t):
                bank = ps[t % 2]
                if t >= 2:
                    pe.wait_ge(S["mask_done"], t - 1)
                for h in range(HEADS):
                    last = pe.matmul(bank[:, h * P:(h + 1) * P], E2[:, h, t * P:(t + 1) * P],
                                     E1[:, h, t * P:(t + 1) * P], start=True, stop=True)
                last.then_inc(S["score_done"], 1)

            scores(0)
            pe.wait_ge(S["kt_copied"], NT)
            for t in range(NT):
                ob = 2 if t % 2 == 0 else 6
                if t + 1 < NT:
                    scores(t + 1)
                for c in range(2):
                    n = 2 * t + c
                    if n == SEQ // CHUNK - 1:
                        break
                    rows_c = slice(CHUNK * c, CHUNK * (c + 1))
                    if n >= 1:
                        pe.wait_ge(S["state_ready"], n)
                    for h in range(HEADS):
                        last = pe.matmul(ps[4 + h // 2][:, (h % 2) * HV:(h % 2 + 1) * HV], KT[rows_c, t, h, :],
                                         VG[rows_c, t, h * HV:(h + 1) * HV], start=True, stop=True)
                    last.then_inc(S["kv_done"], 1)
                pe.wait_ge(S["mask_done"], t + 1)
                if t >= 2:
                    pe.wait_ge(S["o_gated"], t - 1)
                pe.wait_ge(S["state_ready"], 2 * t + 1)
                for h in range(HEADS):
                    dst = ps[ob + h // 2][:, (h % 2) * HV:(h % 2 + 1) * HV]
                    last = pe.matmul(dst, AS[:, t % 2, h, :], VG[:, t, h * HV:(h + 1) * HV], start=True, stop=False,
                                     skip_group_check=True)
                    for c in range(2):
                        n = 2 * t + c
                        if n == 0:
                            continue
                        last = pe.matmul(dst[CHUNK * c:CHUNK * (c + 1), :],
                                         E1[:, h, n * CHUNK:(n + 1) * CHUNK], ST[:, n % 2, h, :],
                                         start=False, stop=c == 1, skip_group_check=True)
                last.then_inc(S["o_done"], 1)

            transposes(1, 0, lambda t, k: SR[:, t, k * P:(k + 1) * P],
                       lambda t: pe.wait_ge(S["o_gated"], max(t + 1, 3 if t == 1 else 0)))
            dense("go0", GO0, 4, 1, lambda j: None)
            dense("go1", GO1, 0, 1, xt_free(1))

            def router(layer, n_xt):
                pe.wait_ge(S["rw_lo"], layer + 1)
                pe.wait_ge(S["xt_lo"], 8 * n_xt + 8)
                for k in range(KD):
                    last = mm3(pe, ps[4][:, :], RWH[:, k, :], RWL[:, k, :], XTH[:, k, :], XTL[:, k, :],
                               k == 0, k == KD - 1)
                last.then_inc(S["logits_formed"], 1)
                pe.wait_ge(S["logits_copied"], layer + 1)
                for t in range(NT):
                    last = pe.transpose(ps[6][:, t * 20:(t + 1) * 20], SG[0:20, t * P:(t + 1) * P], ident[0:20, 0:20])
                last.then_inc(S["router_done"], 1)
                u = UP[layer]
                pe.wait_ge(S["pt_lo"], layer + 1)
                pe.wait_ge(S["lo_ready"], u + 1)
                for c in range(2):
                    for t in range(NT):
                        if c == 1:
                            wait_freed(pe, f"up{layer}0", t)
                        for k in range(2):
                            cols = slice(k * D + c * 512, k * D + (c + 1) * 512)
                            last = mm3(pe, ps[t][:, :], pTH[:, k, t * P:(t + 1) * P], pTL[:, k, t * P:(t + 1) * P],
                                       WH[:, u % SPLIT, cols], WL[:, u % SPLIT, cols], k == 0, k == 1)
                        if c == 1 and t == NT - 1:
                            last.then_inc(S["unit_used"], 1)
                        else:
                            last.then_inc(S["up_done"], 1)
                pe.wait_ge(S["mask16_ready"], layer + 1)
                M = r16[:, 2, :, :]
                for t in range(NT):
                    for b in range(t):
                        pe.matmul(ps[7][:, t * 16:(t + 1) * 16], ones, M[:, b, :], start=b == 0, stop=False)
                    pe.matmul(ps[7][:, t * 16:(t + 1) * 16], before, M[:, t, :], start=t == 0, stop=True)
                for t in range(NT):
                    last = pe.matmul(ps[7][:, 64:80], ones, M[:, t, :], start=t == 0, stop=t == NT - 1)
                last.then_inc(S["rank_done"], 1)
                for t in range(NT):
                    wait_freed(pe, f"up{layer}1", t)
                pe.wait_ge(S["marks_ready"], layer + 1)
                for kt in range(2 * NT):
                    last = pe.matmul(ps[6][:, 128:192], slot_marks[:, kt, :], column_rows[:, kt, :],
                                     start=kt == 0, stop=kt == 2 * NT - 1)
                last.then_inc(S["slots_formed"], 1)

            def gather_transposes(layer, e):
                q = EXPERTS * layer + e
                pe.wait_ge(S["gathered"], 16 * q + 16)
                for half in range(2):
                    if has(e, 1, 99) or layer:
                        pe.wait_ge(S["gx_lo"], 2 * q - 1 + half)
                    for k in range(4):
                        last = pe.transpose(ps[4 + half][:, k * P:(k + 1) * P],
                                            XG[:, (4 * half + k) * P:(4 * half + k + 1) * P], ident)
                    last.then_inc(S["gx_pe"], 1)

            def moe(layer):
                def step(i, _):
                    q = EXPERTS * layer + i
                    u = lambda j: unit_of(layer, i, j)
                    s0 = MOE[layer] + (0 if isinstance(i, int) and i == 0 else -2)
                    if has(i, 0, 0) and isinstance(i, int):
                        gather_transposes(layer, 0)
                    for which in range(2):
                        if has(i, 0, EXPERTS - 1):
                            if not (isinstance(i, int) and i == 0):
                                pe.wait_ge(S["silu_ready" if which == 0 else "glu_ready"], q)
                            if which == 0:
                                pe.wait_ge(S["gx_lo"], 2 * q + 2)
                            for half in range(2):
                                j = 2 * which + half
                                s = (s0 + j) % SPLIT
                                pe.wait_ge(S["lo_ready"], u(j) + 1)
                                for k in range(4):
                                    c = slice(k * 512, (k + 1) * 512)
                                    kk = 4 * half + k
                                    last = mm3(pe, ps[which][:, :], XTH[:, kk, 0:P], XTL[:, kk, 0:P],
                                               WH[:, s, c], WL[:, s, c], half == 0 and k == 0, half == 1 and k == 3)
                                last.then_inc(S["unit_used"], 1)
                        if which == 0 and has(i, 1, EXPERTS):
                            pe.wait_ge(S["glu_ready"], q)
                            if not (isinstance(i, int) and i == 1) or layer:
                                pe.wait_ge(S["at_lo"], q - 1)
                            for k in range(4):
                                last = pe.transpose(ps[6][:, k * P:(k + 1) * P], AG[:, k * P:(k + 1) * P], ident)
                            last.then_inc(S["at_pe"], 1)
                    if has(i, 0, EXPERTS - 2):
                        gather_transposes(layer, i + 1)
                    if has(i, 1, EXPERTS):
                        pe.wait_ge(S["at_lo"], q)
                        if has(i, 2, 99) or layer:
                            pe.wait_ge(S["y_act"], q - 1)
                            pe.wait_ge(S["y_dve"], q - 1)
                        for half in range(2):
                            j = (0 if isinstance(i, int) and i == EXPERTS else 4) + half
                            s = (s0 + j) % SPLIT
                            pe.wait_ge(S["lo_ready"], u(j) + 1)
                            for k in range(4):
                                c = slice(k * 512, (k + 1) * 512)
                                last = mm3(pe, ps[2 + half][:, :], ATH[:, k, :], ATL[:, k, :],
                                           WH[:, s, c], WL[:, s, c], k == 0, k == 3)
                            last.then_inc(S["unit_used"], 1)
                moe_steps(pe, layer, None, step)
                pe.wait_ge(S["y_act"], EXPERTS * (layer + 1))
                pe.wait_ge(S["y_dve"], EXPERTS * (layer + 1))
                overflow(pe, layer, overflow_pe)

            def overflow_pe(n, v):
                pe.wait_ge(v["gathered"], 16 * n + 16)
                for half in range(2):
                    for k in range(4):
                        last = pe.transpose(ps[4 + half][:, k * P:(k + 1) * P],
                                            XG[:, (4 * half + k) * P:(4 * half + k + 1) * P], ident)
                    last.then_inc(v["x_pe"], 1)
                pe.wait_ge(v["x_copied"], 2 * n + 2)
                for j in range(4):
                    pe.wait_ge(v[f"weights{j % 2}"], 48 * n + 16 * (j // 2 + 1))
                    for k in range(4):
                        last = pe.matmul(ps[j // 2][:, :], XO[:, 4 * (j % 2) + k, :],
                                         WOV[:, j % 2, k * 512:(k + 1) * 512],
                                         start=j % 2 == 0 and k == 0, stop=j % 2 == 1 and k == 3)
                    last.then_inc(v["used"], 1)
                pe.wait_ge(v["glu"], n + 1)
                for k in range(4):
                    last = pe.transpose(ps[6][:, k * P:(k + 1) * P], AG[:, k * P:(k + 1) * P], ident)
                last.then_inc(v["a_pe"], 1)
                pe.wait_ge(v["a_copied"], n + 1)
                for j in range(2):
                    pe.wait_ge(v[f"weights{j}"], 48 * n + 48)
                    for k in range(4):
                        last = pe.matmul(ps[2 + j][:, :], AO[:, k, :], WOV[:, j, k * 512:(k + 1) * 512],
                                         start=k == 0, stop=k == 3)
                    last.then_inc(v["used"], 1)

            def ple(layer, n_xt):
                transposes(n_xt, 4, hn, rows(2 if layer == 0 else 5))
                dense(f"pg{layer}0", PG[layer], 0, n_xt, lambda j: None)
                dense(f"pg{layer}1", PG[layer] + 2, 4, n_xt, xt_free(n_xt))

            for j in range(4):
                wait_freed(pe, "go0", j)
            transposes(2, 4, hn, rows(1))
            for j in range(4):
                wait_freed(pe, "go1", j)
            router(0, 2)
            moe(0)
            ple(0, 3)

            for j in range(4):
                wait_freed(pe, "pg00", j)
            transposes(4, 0, hn, rows(3))
            dense("sv0", SV[0], 4, 4, after("pg01"))
            dense("sv1", SV[1], 0, 4, xt_free(4))
            dense("sv2", SV[2], 4, 4, after("sv0"))
            dense("sv3", SV[3], 0, 4, after("sv1"))
            for c in range(4):
                dense(f"su{c}", SU[c], 4, 4, after("sv2" if c == 0 else f"su{c - 1}"))
                pe.wait_ge(S["ln_done"], NT if c < 2 else 2 * NT)
                for t in range(NT):
                    if c == 0:
                        wait_freed(pe, "sv3", t)
                    else:
                        pe.wait_ge(S["prod_done"], 8 * (c - 1) + 2 * t + 2)
                    for gg in range(2):
                        g = 2 * c + gg
                        last = pe.matmul(ps[t][:, gg * 256:(gg + 1) * 256], WST[:, g, :],
                                         VS[:, t, g * 256:(g + 1) * 256], start=True, stop=True)
                    last.then_inc(S["s_done"], 1)
            for half in range(2):
                n = 5 + half
                if half == 0:
                    for j in range(4):
                        wait_freed(pe, "su3", j)
                    ready = lambda t: pe.wait_ge(S["prod_done"], 16)
                else:
                    for j in range(4):
                        wait_freed(pe, "so00", j)
                    ready = lambda t: pe.wait_ge(S["prod_done"], 32)
                base = 4 if half == 0 else 0
                transposes(n, base, lambda t, k, half=half: VS[:, t, half * D + k * P:half * D + (k + 1) * P], ready)
                dense(f"so{half}0", SO[half][0], 4 - base, n,
                      (lambda j: pe.wait_ge(S["prod_done"], 32)) if half == 0 else after("so01"))
                dense(f"so{half}1", SO[half][1], base, n, xt_free(n))
            for j in range(4):
                wait_freed(pe, "so10", j)
            transposes(7, 4, hn, rows(4))
            for j in range(4):
                wait_freed(pe, "so11", j)
            router(1, 7)
            moe(1)
            ple(1, 8)

        @block.scalar
        def _(act):
            split = Splitter(act, True)
            steps = [0]

            def link(ins):
                steps[0] += 1
                ins.then_inc(S["act_chain"], 1)
                act.wait_ge(S["act_chain"], steps[0])

            def stat(m, t, ready, junk):
                ready(t)
                if m:
                    act.wait_ge(S["rows_ready"], 4 * m)
                link(act.activation(junk, H[:, t, :], ACT.Square, accum_out=square_sum[:, t:t + 1]))
                act.activation(root[:, t:t + 1], square_sum[:, t:t + 1], ACT.Sqrt, bias=EPS, scale=1.0 / D)\
                    .then_inc(S["rms_ready"], 1)

            def high(n, base, t):
                for half in range(2):
                    act.wait_ge(S["xt_pe"], 8 * n + 2 * t + half + 1)
                    src = ps[base + 2 * (t % 2) + half][:, :].rearrange("p (k s) -> p k s", k=4)
                    act.activation(XTH[:, 4 * half:4 * half + 4, t * P:(t + 1) * P], src, ACT.Copy)\
                        .then_inc(S["xt_hi"], 1)

            def norm_phase(n, base, m, ready, junk):
                stat(m, 0, ready, junk)
                stat(m, 1, ready, junk)
                for t in range(NT):
                    high(n, base, t)
                    if t + 2 < NT:
                        stat(m, t + 2, ready, junk)

            def dense_out(name, u0, base, body):
                split.to(u0 + AHEAD)
                split.to(u0 + 1 + AHEAD)
                for j in range(4):
                    wait_tile(act, name, u0 + 1, j)
                    body(j, ps[base + j]).then_inc(S["freed_act"], 1)

            act.wait_ge(S["misc_loaded"], MISC)
            act.activation(WAH[:, :, :], rwa[:, :, :], ACT.Copy).then_inc(S["early_split_hi"], 1)
            split.to(1)
            junk1 = E1[:, 0:2, :].rearrange("p a s -> p (a s)")
            norm_phase(0, 0, 0, lambda t: act.wait_ge(S["x_loaded"], 16), junk1)

            act.wait_ge(S["a_done"], 1)
            act.activation(aT[:, :], ps[4][:, :], ACT.Copy).then_inc(S["a_copied"], 1)

            def softplus(h):
                act.wait_ge(S["z_done"], h + 1)
                bias = small[:, S_BG + h:S_BG + h + 1]
                act.activation(E1[:, h, :], ps[4 + h][:, :], ACT.Abs, bias=bias).then_inc(S["abs_read"], 1)
                act.wait_ge(S["abs_read"], h + 1)
                link(act.activation(E1[:, h, :], E1[:, h, :], ACT.Exp, scale=-1.0))
                act.activation(E1[:, h, :], E1[:, h, :], ACT.Ln, bias=1.0).then_inc(S["decay_act"], 1)

            def decays(h):
                act.wait_ge(S["bc_ready"], h + 1)
                act.activation(E1[:, h, :], bcum[:, h % 2, :], ACT.Exp, scale=1.0 / TAU)
                act.activation(E2[:, h, :], bcum[:, h % 2, :], ACT.Exp, scale=-1.0 / TAU)
                act.wait_ge(S["dlt_ready"], h + 1)
                act.activation(E3[:, h, :], E3[:, h, :], ACT.Exp, scale=1.0 / TAU).then_inc(S["e_ready"], 1)

            def copy_v(c):
                return lambda j, bank: act.activation(VG[:, j, c * 512:(c + 1) * 512], bank[:, :], ACT.Copy)

            def silu_r(c):
                return lambda j, bank: act.activation(SR[:, j, c * 512:(c + 1) * 512], bank[:, :], ACT.Silu)

            split.to(V0 + 1 + AHEAD)
            for h in range(HEADS):
                softplus(h)
                if h >= 1:
                    decays(h - 1)
                if h == 0:
                    for j in range(4):
                        wait_tile(act, "v0", V0 + 1, j)
                        copy_v(0)(j, ps[j]).then_inc(S["freed_act"], 1)
            decays(HEADS - 1)
            split.to(Q + AHEAD)
            split.to(K + AHEAD)
            dense_out("v1", V1, 0, copy_v(1))
            dense_out("r0", R0, 4, silu_r(0))
            dense_out("r1", R1, 0, silu_r(1))
            act.wait_ge(S["kt_done"], NT)
            KT = E3[:, :, :].rearrange("p h s -> p (h s)").rearrange("p (t f) -> p t f", t=NT)
            for t in range(NT):
                act.activation(KT[:, t, :], ps[4 + t][:, :], ACT.Copy).then_inc(S["kt_copied"], 1)
            for t in range(NT):
                act.wait_ge(S["o_done"], t + 1)
                if t:
                    act.wait_ge(S["o_gated"], t)
                ob = 2 if t % 2 == 0 else 6
                for h in range(HEADS):
                    src = ps[ob + h // 2][:, (h % 2) * HV:(h % 2 + 1) * HV]
                    link(act.activation(o_junk[:, :], src, ACT.Square, accum_out=oss[:, 0, h:h + 1]))
                act.activation(oss[:, 1, :], oss[:, 0, :], ACT.Sqrt, bias=EPS, scale=1.0 / HV).then_inc(S["o_root"], 1)
            for t in range(NT):
                high(1, 0, t)
            def split_router(layer):
                act.wait_ge(S["rw_loaded"], 16 * layer + 16)
                act.activation(RWH[:, :, :], rw[:, :, :], ACT.Copy).then_inc(S["rw_hi"], 1)

            split.to(GO0 + 1 + AHEAD)
            split_router(0)
            split.to(GO1 + 1 + AHEAD)

            def split_p(layer):
                act.wait_ge(S["pt_loaded"], 16 * layer + 16)
                act.activation(pTH[:, :, :], pT[:, :, :], ACT.Copy).then_inc(S["pt_hi"], 1)

            def route(layer):
                act.wait_ge(S["logits_formed"], layer + 1)
                act.activation(SG[0:20, :], ps[4][0:20, :], ACT.Copy).then_inc(S["logits_copied"], 1)
                split.to(UP[layer] + AHEAD)
                act.wait_ge(S["exp_in"], 2 * layer + 1)
                act.activation(r4[:, 1, :, :], r4[:, 0, :, :], ACT.Exp).then_inc(S["exp_out"], 1)

                def up(c, t):
                    if c == 1 and t == NT - 1:
                        act.wait_ge(S["unit_used"], UP[layer] + 1)
                    else:
                        act.wait_ge(S["up_done"], 7 * layer + 4 * c + t + 1)
                    act.activation(PU[:, t, c * 512:(c + 1) * 512], ps[t][:, :], ACT.Copy)\
                        .then_inc(S["freed_act"], 1)
                for t in range(NT):
                    up(0, t)
                act.wait_ge(S["exp_in"], 2 * layer + 2)
                act.activation(r1t[:, 3, :], r1t[:, 2, :], ACT.Exp).then_inc(S["exp_out"], 1)
                for t in range(NT):
                    up(1, t)

            def moe(layer):
                def step(i, split_to):
                    q = EXPERTS * layer + i
                    jmax = 3 if isinstance(i, int) and i == 0 else 1 if isinstance(i, int) and i == EXPERTS else 5
                    if isinstance(i, int) and i > EXPERTS:
                        jmax = -1
                    last_step = isinstance(i, int) and i == EXPERTS

                    def ahead(*js):
                        for j in js:
                            if j <= jmax:
                                split_to(j)

                    if isinstance(i, int) and i == 0:
                        gather_high(layer, 0)
                    if has(i, 2, EXPERTS + 1):
                        act.wait_ge(S["unit_used"], last_down(layer, i - 2) + 1)
                        if not (isinstance(i, int) and i == 2 and layer == 0):
                            y_free(act, q - 2, i)
                        act.activation(Y[:, 0:512], ps[2][:, :], ACT.Copy).then_inc(S["y_act"], 1)
                    if not last_step:
                        ahead(0, 1)
                    if has(i, 1, EXPERTS):
                        act.wait_ge(S["at_pe"], q)
                        act.activation(ATH[:, :, :], ps[6][:, :].rearrange("p (k s) -> p k s", k=4), ACT.Copy)\
                            .then_inc(S["at_hi"], 1)
                    if has(i, 0, EXPERTS - 1):
                        act.wait_ge(S["unit_used"], unit_of(layer, i, 1) + 1)
                        if has(i, 1, 99) or layer:
                            if not (isinstance(i, int) and i == 0 and layer == 0):
                                act.wait_ge(S["glu_ready"], q)
                        act.activation(SG[:, :], ps[0][:, :], ACT.Silu).then_inc(S["silu_ready"], 1)
                    ahead(*((0, 1) if last_step else (2, 3)))
                    if has(i, 0, EXPERTS - 2):
                        gather_high(layer, i + 1)
                    ahead(4, 5)
                moe_steps(act, layer, split, step)

                overflow(act, layer, overflow_act)

            def overflow_act(n, v):
                gate_unit = act.value_load(extra_i[0:1, 2, bass.ds(n, 1)], min_val=0, max_val=UNITS - 4)
                down_unit = act.value_load(extra_i[0:1, 3, bass.ds(n, 1)], min_val=0, max_val=UNITS - 2)

                def load(j):
                    u = gate_unit + j if j < 4 else down_unit + (j - 4)
                    if j >= 2:
                        act.wait_ge(v["used"], 6 * n + j - 1)
                    act.dma_start(WOV[:, j % 2, :], weight_stream[bass.ds(u, 1)].rearrange("u p f -> p (u f)"))\
                        .then_inc(v[f"weights{j % 2}"], 16)

                load(0)
                load(1)
                for half in range(2):
                    act.wait_ge(v["x_pe"], 2 * n + half + 1)
                    act.activation(XO[:, 4 * half:4 * half + 4, :],
                                   ps[4 + half][:, :].rearrange("p (k s) -> p k s", k=4), ACT.Copy)\
                        .then_inc(v["x_copied"], 1)
                load(2)
                load(3)
                act.activation(SG[:, :], ps[0][:, :], ACT.Silu).then_inc(v["silu"], 1)
                load(4)
                load(5)
                act.wait_ge(v["a_pe"], n + 1)
                act.activation(AO[:, :, :], ps[6][:, :].rearrange("p (k s) -> p k s", k=4), ACT.Copy)\
                    .then_inc(v["a_copied"], 1)
                act.wait_ge(v["used"], 6 * n + 6)
                for half in range(2):
                    act.activation(Y[:, half * 512:(half + 1) * 512], ps[2 + half][:, :], ACT.Copy)\
                        .then_inc(v["y"], 1)

            def gather_high(layer, e):
                q = EXPERTS * layer + e
                for half in range(2):
                    act.wait_ge(S["gx_pe"], 2 * q + half + 1)
                    act.activation(XTH[:, 4 * half:4 * half + 4, 0:P],
                                   ps[4 + half][:, :].rearrange("p (k s) -> p k s", k=4), ACT.Copy)\
                        .then_inc(S["gx_hi"], 1)

            def ple(layer, n, m):
                norm_phase(n, 4, m, lambda t: act.wait_ge(S["combined"], 4 * layer + t + 1), junk3[:, :])
                for c in range(2):
                    def body(j, bank, c=c):
                        if c == 1:
                            act.wait_ge(S["ple_added"], 8 * layer + j + 1)
                        return act.activation(GT[:, j, :], bank[:, :], ACT.Sigmoid)
                    dense_out(f"pg{layer}{c}", PG[layer] + 2 * c, 4 * c, body)

            norm_phase(2, 4, 1, lambda t: wait_freed(act, "go1", t), junk3[:, :])
            split_p(0)
            route(0)
            moe(0)
            ple(0, 3, 2)

            norm_phase(4, 0, 3, lambda t: act.wait_ge(S["ple_added"], 4 + t + 1), junk3[:, :])
            for c in range(4):
                def gelu_v(j, bank, c=c):
                    return act.activation(VS[:, j, c * 512:(c + 1) * 512], bank[:, :], ACT.Gelu_apprx_tanh,
                                          accum_out=vsum[:, j, c:c + 1])
                dense_out(f"sv{c}", SV[c], 4 if c % 2 == 0 else 0, gelu_v)
            split.to(SU[0] + AHEAD)
            for t in range(NT):
                act.wait_ge(S["mean_ready"], t + 1)
                link(act.activation(UT[:, :, :].rearrange("p a n -> p (a n)"), VS[:, t, :], ACT.Square,
                                    bias=vst[:, 1, t:t + 1], accum_out=vst[:, 2, t:t + 1]))
                act.activation(vst[:, 3, t:t + 1], vst[:, 2, t:t + 1], ACT.Sqrt, bias=EPS, scale=1.0 / (2 * D))\
                    .then_inc(S["ln_root"], 1)
            for c in range(4):
                def gelu_u(j, bank, c=c):
                    if c:
                        act.wait_ge(S["prod_done"], 8 * (c - 1) + 2 * j + 2)
                    return act.activation(UT[:, j, :], bank[:, :], ACT.Gelu_apprx_tanh)
                dense_out(f"su{c}", SU[c], 4, gelu_u)
            for half in range(2):
                for t in range(NT):
                    high(5 + half, 4 if half == 0 else 0, t)
                for c in range(2):
                    split.to(SO[half][c] + AHEAD)
                    split.to(SO[half][c] + 1 + AHEAD)
                    if half == 1 and c == 0:
                        split_router(1)
            norm_phase(7, 4, 4, lambda t: wait_freed(act, "so11", t), junk3[:, :])
            split_p(1)
            route(1)
            moe(1)
            ple(1, 8, 5)
            for t in range(NT):
                stat(6, t, lambda t: act.wait_ge(S["ple_added"], 12 + t + 1), junk3[:, :])

        @block.vector
        def _(dve):
            split = Splitter(dve, False)
            steps = [0]

            def link(ins):
                steps[0] += 1
                ins.then_inc(S["dve_chain"], 1)
                dve.wait_ge(S["dve_chain"], steps[0])

            def norm(m, n, t, store, gain_no, out_of=None):
                dve.wait_ge(S["rms_ready"], 4 * m + t + 1)
                link(dve.reciprocal(rstd[:, t:t + 1], root[:, t:t + 1]))
                dve.wait_ge(S["gain_loaded"], 16 * gain_no + 16)
                if n is not None:
                    if t >= 2:
                        dve.wait_ge(S["xt_pe"], 8 * n + 2 * (t - 2) + 2)
                        if store is not None:
                            dve.wait_ge(hn_stored[t % 2], 32 * store + 16)
                    dve.scalar_tensor_tensor(out=HN[:, t % 2, :], in0=H[:, t, :], scalar=rstd[:, t:t + 1],
                                             in1=gain[:, :], op0=ALU.mult, op1=ALU.mult)\
                        .then_inc(S["rows_ready"], 1)
                else:
                    dve.scalar_tensor_tensor(out=H[:, t, :], in0=H[:, t, :], scalar=rstd[:, t:t + 1],
                                             in1=gain[:, :], op0=ALU.mult, op1=ALU.mult)\
                        .then_inc(S["out_ready"], 1)

            def low(n, base, t):
                for half in range(2):
                    dve.wait_ge(S["xt_hi"], 8 * n + 2 * t + half + 1)
                    src = ps[base + 2 * (t % 2) + half][:, :].rearrange("p (k s) -> p k s", k=4)
                    at = (slice(None), slice(4 * half, 4 * half + 4), slice(t * P, (t + 1) * P))
                    dve.tensor_tensor(XTL[at], src, XTH[at], ALU.subtract).then_inc(S["xt_lo"], 1)

            def norm_phase(n, base, m, gain_no, store=None):
                norm(m, n, 0, store, gain_no)
                norm(m, n, 1, store, gain_no)
                for t in range(NT):
                    low(n, base, t)
                    if t + 2 < NT:
                        norm(m, n, t + 2, store, gain_no)

            def add_out(name, u0, base, c):
                split.to(u0 + AHEAD)
                split.to(u0 + 1 + AHEAD)
                for j in range(4):
                    wait_tile(dve, name, u0 + 1, j)
                    at = H[:, j, c * 512:(c + 1) * 512]
                    dve.tensor_tensor(at, ps[base + j][:, :], at, ALU.add).then_inc(S["freed_dve"], 1)

            dve.wait_ge(S["early_split_hi"], 1)
            dve.tensor_tensor(WAL[:, :, :], rwa[:, :, :], WAH[:, :, :], ALU.subtract).then_inc(S["early_split_lo"], 1)
            split.to(1)
            norm_phase(0, 0, 0, 0)

            split.to(V0 + 1 + AHEAD)
            for h in range(HEADS):
                bias = small[:, S_BG + h:S_BG + h + 1]
                dve.wait_ge(S["z_done"], h + 1)
                dve.wait_ge(S["abs_read"], h + 1)
                link(dve.tensor_scalar(E2[:, h, :], ps[4 + h][:, :], bias, 0.0, ALU.add, ALU.min))
                dve.wait_ge(S["decay_act"], h + 1)
                dve.tensor_tensor(E2[:, h, :], E2[:, h, :], E1[:, h, :], ALU.subtract).then_inc(S["z_read"], 1)
                dve.wait_ge(S["z_read"], h + 1)
                if h >= 2:
                    dve.wait_ge(S["e_ready"], h - 1)
                dve.tensor_tensor_scan(bcum[:, h % 2, :], scan_mask[:, :], E2[:, h, :], 0.0, ALU.mult, ALU.add)\
                    .then_inc(S["bc_ready"], 1)
                dve.wait_ge(S["bc_ready"], h + 1)
                b3 = bcum[:, h % 2, :].rearrange("p (n i) -> p n i", i=CHUNK)
                dve.tensor_tensor(E3[:, h, :].rearrange("p (n i) -> p n i", i=CHUNK),
                                  b3[:, :, CHUNK - 1:CHUNK].broadcast_to([P, SEQ // CHUNK, CHUNK]), b3,
                                  ALU.subtract).then_inc(S["dlt_ready"], 1)
            split.to(Q + AHEAD)
            split.to(Q + 1 + AHEAD)
            for h in range(HEADS):
                dve.wait_ge(S["e_ready"], h + 1)
                link(dve.tensor_copy(chunk_decay[:, h, :],
                                     E1[:, h, :].rearrange("p (n i) -> p n i", i=CHUNK)[:, :, CHUNK - 1]))
                wait_tile(dve, "q", Q + 1, h)
                dve.scalar_tensor_tensor(out=E1[:, h, :], in0=ps[h][:, :], scalar=float(P) ** -0.5, in1=E1[:, h, :],
                                         op0=ALU.mult, op1=ALU.mult).then_inc(S["freed_dve"], 1)
            split.to(K + AHEAD)
            split.to(K + 1 + AHEAD)
            for h in range(HEADS):
                wait_tile(dve, "k", K + 1, h)
                dve.tensor_tensor(E2[:, h, :], ps[4 + h][:, :], E2[:, h, :], ALU.mult)
                dve.tensor_tensor(E3[:, h, :], ps[4 + h][:, :], E3[:, h, :], ALU.mult)\
                    .then_inc(S["freed_dve"], 1)
            for u in range(V1, R1 + 2):
                split.to(u + AHEAD)
            dve.wait_ge(S["gain_loaded"], 32)
            for t in range(NT):
                wait_freed(dve, "r1", t)
                dve.tensor_tensor(SR[:, t, :], SR[:, t, :], gain[:, :], ALU.mult).then_inc(S["sr_scaled"], 1)

            def mask(t):
                dve.wait_ge(S["score_done"], t + 1)
                if t >= 2:
                    dve.wait_ge(S["o_done"], t - 1)
                dve.tensor_tensor(AS[:, t % 2, :, :], ps[t % 2][:, :].rearrange("p (h i) -> p h i", h=HEADS),
                                  chunk_mask.unsqueeze(1).broadcast_to([P, HEADS, P]), ALU.mult)\
                    .then_inc(S["mask_done"], 1)

            def split_router(layer):
                dve.wait_ge(S["rw_hi"], layer + 1)
                dve.tensor_tensor(RWL[:, :, :], rw[:, :, :], RWH[:, :, :], ALU.subtract).then_inc(S["rw_lo"], 1)

            mask(0)
            for t in range(NT):
                if t + 1 < NT:
                    mask(t + 1)
                for c in range(2):
                    n = 2 * t + c
                    if n == SEQ // CHUNK - 1:
                        break
                    dve.wait_ge(S["kv_done"], n + 1)
                    if n:
                        dve.wait_ge(S["state_ready"], n)
                        dve.wait_ge(S["o_done"], (n - 1) // 2 + 1)
                    for h in range(HEADS):
                        kv = ps[4 + h // 2][:, (h % 2) * HV:(h % 2 + 1) * HV]
                        if n == 0:
                            last = dve.tensor_copy(ST[:, 1, h, :], kv)
                        else:
                            last = dve.scalar_tensor_tensor(
                                out=ST[:, (n + 1) % 2, h, :], in0=ST[:, n % 2, h, :],
                                scalar=chunk_decay[:, h, n:n + 1], in1=kv, op0=ALU.mult, op1=ALU.add)
                    last.then_inc(S["state_ready"], 1)
                dve.wait_ge(S["o_root"], t + 1)
                link(dve.reciprocal(oss[:, 2, :], oss[:, 1, :]))
                dve.wait_ge(S["sr_scaled"], t + 1)
                ob = 2 if t % 2 == 0 else 6
                for h in range(HEADS):
                    at = SR[:, t, h * HV:(h + 1) * HV]
                    last = dve.scalar_tensor_tensor(out=at, in0=ps[ob + h // 2][:, (h % 2) * HV:(h % 2 + 1) * HV],
                                                    scalar=oss[:, 2, h:h + 1], in1=at, op0=ALU.mult, op1=ALU.mult)
                last.then_inc(S["o_gated"], 1)
                dve.wait_ge(S["o_gated"], t + 1)
            for t in range(NT):
                low(1, 0, t)
            add_out("go0", GO0, 4, 0)
            split_router(0)
            add_out("go1", GO1, 0, 1)

            def split_p(layer):
                dve.wait_ge(S["pt_hi"], layer + 1)
                dve.tensor_tensor(pTL[:, :, :], pT[:, :, :], pTH[:, :, :], ALU.subtract).then_inc(S["pt_lo"], 1)

            def route(layer):
                split.to(UP[layer] + AHEAD)
                L4 = [P, NT, 4]
                dve.wait_ge(S["router_done"], layer + 1)
                bias = small[:, S_RB + 80 * layer:S_RB + 80 * (layer + 1)].rearrange("p (t n) -> p t n", t=NT)
                link(dve.tensor_tensor(lg[:, :, :], ps[6][:, 0:80].rearrange("p (t n) -> p t n", t=NT), bias, ALU.add))
                group = lg[:, :, 0:4]

                def top(values, best, onehot, scratch):
                    link(dve.tensor_reduce(r1t[:, best, :], values, AX.X, ALU.max))
                    link(dve.tensor_tensor(r4[:, onehot, :, :], values,
                                           r1t[:, best, :].unsqueeze(2).broadcast_to(L4), ALU.is_equal))
                    link(dve.tensor_tensor(r4[:, onehot, :, :], r4[:, onehot, :, :], tie, ALU.mult))
                    link(dve.tensor_reduce(r1t[:, scratch, :], r4[:, onehot, :, :], AX.X, ALU.max))
                    link(dve.tensor_tensor(r4[:, onehot, :, :], r4[:, onehot, :, :],
                                           r1t[:, scratch, :].unsqueeze(2).broadcast_to(L4), ALU.is_equal))

                top(group, 0, 2, 1)
                dve.tensor_tensor(r4[:, 0, :, :], group, r1t[:, 0, :].unsqueeze(2).broadcast_to(L4), ALU.subtract)\
                    .then_inc(S["exp_in"], 1)
                L16 = [P, NT, 4, 4]
                v44 = lambda k: r16[:, k, :, :].rearrange("p t (g e) -> p t g e", g=4)
                chosen = r4[:, 2, :, :].unsqueeze(3).broadcast_to(L16)
                link(dve.tensor_tensor(v44(0), lg[:, :, 4:20].rearrange("p t (g e) -> p t g e", g=4), chosen,
                                       ALU.mult))
                link(dve.tensor_reduce(r4[:, 3, :, :], r16[:, 0, :, :].rearrange("p t (g e) -> p t e g", g=4),
                                       AX.X, ALU.add))
                top(r4[:, 3, :, :], 4, 4, 1)
                link(dve.scalar_tensor_tensor(out=r4[:, 5, :, :], in0=r4[:, 4, :, :], scalar=FAR, in1=r4[:, 3, :, :],
                                              op0=ALU.mult, op1=ALU.add))
                top(r4[:, 5, :, :], 5, 6, 1)
                dve.tensor_tensor(r1t[:, 2, :], r1t[:, 5, :], r1t[:, 4, :], ALU.subtract).then_inc(S["exp_in"], 1)
                link(dve.tensor_tensor(v44(1), chosen, r4[:, 4, :, :].unsqueeze(2).broadcast_to(L16), ALU.mult))
                link(dve.tensor_tensor(v44(3), chosen, r4[:, 6, :, :].unsqueeze(2).broadcast_to(L16), ALU.mult))
                dve.tensor_tensor(r16[:, 2, :, :], r16[:, 1, :, :], r16[:, 3, :, :], ALU.add)\
                    .then_inc(S["mask16_ready"], 1)
                dve.wait_ge(S["exp_out"], 2 * layer + 2)
                link(dve.tensor_reduce(r1t[:, 6, :], r4[:, 1, :, :], AX.X, ALU.add))
                link(dve.tensor_scalar(r1t[:, 7, :], r1t[:, 3, :], 1.0, None, ALU.add))
                link(dve.tensor_tensor(r1t[:, 8, :], r1t[:, 6, :], r1t[:, 7, :], ALU.mult))
                link(dve.reciprocal(w_tok[:, 0, :], r1t[:, 8, :]))
                link(dve.tensor_tensor(w_tok[:, 1, :], w_tok[:, 0, :], r1t[:, 3, :], ALU.mult))
                for k, mask_k in enumerate((1, 3)):
                    link(dve.tensor_tensor(r16[:, 5, :, :], r16[:, mask_k, :, :], eoff, ALU.mult))
                    link(dve.tensor_reduce(place[:, 1, k, :], r16[:, 5, :, :], AX.X, ALU.add))
                dve.wait_ge(S["rank_done"], layer + 1)
                rank_all = ps[7][:, 0:64].rearrange("p (t e) -> p t e", t=NT)
                for k, mask_k in enumerate((1, 3)):
                    link(dve.tensor_tensor(r16[:, 4 + k, :, :], r16[:, mask_k, :, :], rank_all, ALU.mult))
                link(dve.tensor_reduce(place[:, 0, :, :], r16[:, 4:6, :, :], AX.X, ALU.add))
                rank, expert, rnd, slot, column = (place[:, k, :, :] for k in range(5))
                link(dve.tensor_scalar(rnd, rank, float(P), None, ALU.is_ge))
                for k in range(2, ROUNDS):
                    link(dve.scalar_tensor_tensor(out=rnd, in0=rank, scalar=float(k * P), in1=rnd,
                                                  op0=ALU.is_ge, op1=ALU.add))
                link(dve.scalar_tensor_tensor(out=slot, in0=rnd, scalar=float(-P), in1=rank,
                                              op0=ALU.mult, op1=ALU.add))
                link(dve.scalar_tensor_tensor(out=column, in0=rnd, scalar=float(EXPERTS), in1=expert,
                                              op0=ALU.mult, op1=ALU.add))
                flat = lambda v: v.rearrange("p k t -> p (k t)")
                marks, columns = [P, 2 * NT, P], [P, 2 * NT, ROUNDS * EXPERTS]
                link(dve.tensor_tensor(slot_marks, iota.unsqueeze(1).broadcast_to(marks),
                                       flat(slot).unsqueeze(2).broadcast_to(marks), ALU.is_equal))
                link(dve.tensor_tensor(column_rows, iota[:, 0:ROUNDS * EXPERTS].unsqueeze(1).broadcast_to(columns),
                                       flat(column).unsqueeze(2).broadcast_to(columns), ALU.is_equal))
                dve.tensor_tensor(column_rows, column_rows, row_number.unsqueeze(2).broadcast_to(columns), ALU.mult)\
                    .then_inc(S["marks_ready"], 1)
                dve.wait_ge(S["slots_formed"], layer + 1)
                table, far = ps[6][:, 128:192], r16[:, 4, :, :].rearrange("p t e -> p (t e)")
                link(dve.tensor_scalar(far, table, 0.0, float(BIG), ALU.is_equal, ALU.mult))
                link(dve.scalar_tensor_tensor(out=far, in0=table, scalar=-1.0, in1=far, op0=ALU.add, op1=ALU.add))
                link(dve.tensor_copy(slot_rows[:, :], far))
                dve.tensor_scalar(slot_tokens[:, :], slot_rows[:, :], 1, None, ALU.logical_shift_right)\
                    .then_inc(S["slots_ready"], 1)
                list_extra(layer)

            def list_extra(layer):
                full = [P, EXTRA, ROUNDS * EXPERTS]
                need, number = r16[:, 0, :, :], r16[:, 1, :, :].rearrange("p r e -> p (r e)")
                need_flat = need.rearrange("p r e -> p (r e)")
                pick = junk3[:, 0:EXTRA * ROUNDS * EXPERTS].rearrange("p (k n) -> p k n", k=EXTRA)
                entry = junk3[:, 512:512 + EXTRA * ROUNDS * EXPERTS].rearrange("p (k n) -> p k n", k=EXTRA)
                link(dve.memset(need[:, 0, :], 0.0))
                for r in range(1, ROUNDS):
                    link(dve.tensor_scalar(need[:, r, :], ps[7][:, 64:80], float(r * P), None, ALU.is_gt))
                link(dve.tensor_tensor_scan(number, ones[:, 0:ROUNDS * EXPERTS], need_flat, 0.0, ALU.mult, ALU.add))
                link(dve.tensor_tensor(pick, number.unsqueeze(1).broadcast_to(full),
                                       numbers.unsqueeze(2).broadcast_to(full), ALU.is_equal))
                link(dve.tensor_tensor(pick, pick, need_flat.unsqueeze(1).broadcast_to(full), ALU.mult))
                for k in range(3):
                    link(dve.tensor_tensor(entry, pick, tables[:, k, :].unsqueeze(1).broadcast_to(full), ALU.mult))
                    link(dve.tensor_reduce(extra_f[:, 1 + k, 0:EXTRA], entry, AX.X, ALU.add))
                if layer:
                    link(dve.tensor_scalar(extra_f[:, 2:4, 0:EXTRA], extra_f[:, 2:4, 0:EXTRA],
                                           float(MOE[1] - MOE[0]), None, ALU.add))
                link(dve.tensor_copy(extra_i[:, 1:4, 0:EXTRA], extra_f[:, 1:4, 0:EXTRA]))
                dve.tensor_copy(extra_i[:, 0, 0:1], number[:, ROUNDS * EXPERTS - 1:ROUNDS * EXPERTS])\
                    .then_inc(S["extra_ready"], 1)

            def gather_low(layer, e):
                q = EXPERTS * layer + e
                for half in range(2):
                    dve.wait_ge(S["gx_hi"], 2 * q + half + 1)
                    at = (slice(None), slice(4 * half, 4 * half + 4), slice(0, P))
                    dve.tensor_tensor(XTL[at], ps[4 + half][:, :].rearrange("p (k s) -> p k s", k=4), XTH[at],
                                      ALU.subtract).then_inc(S["gx_lo"], 1)

            def moe(layer):
                def step(i, split_to):
                    q = EXPERTS * layer + i
                    jmax = 3 if isinstance(i, int) and i == 0 else 1 if isinstance(i, int) and i == EXPERTS else 5
                    if isinstance(i, int) and i > EXPERTS:
                        jmax = -1
                    last_step = isinstance(i, int) and i == EXPERTS

                    def ahead(*js):
                        for j in js:
                            if j <= jmax:
                                split_to(j)

                    if isinstance(i, int) and i == 0:
                        gather_low(layer, 0)
                    if has(i, 2, EXPERTS + 1):
                        dve.wait_ge(S["unit_used"], last_down(layer, i - 2) + 1)
                        if not (isinstance(i, int) and i == 2 and layer == 0):
                            y_free(dve, q - 2, i)
                        dve.tensor_copy(Y[:, 512:D], ps[3][:, :]).then_inc(S["y_dve"], 1)
                    if not last_step:
                        ahead(0, 1)
                    if has(i, 1, EXPERTS):
                        dve.wait_ge(S["at_hi"], q)
                        dve.tensor_tensor(ATL[:, :, :], ps[6][:, :].rearrange("p (k s) -> p k s", k=4),
                                          ATH[:, :, :], ALU.subtract).then_inc(S["at_lo"], 1)
                    ahead(*((0, 1) if last_step else (2, 3)))
                    if has(i, 0, EXPERTS - 1):
                        dve.wait_ge(S["silu_ready"], q + 1)
                        dve.wait_ge(S["unit_used"], unit_of(layer, i, 3) + 1)
                        dve.tensor_tensor(AG[:, :], ps[1][:, :], SG[:, :], ALU.mult).then_inc(S["glu_ready"], 1)
                    if has(i, 0, EXPERTS - 2):
                        gather_low(layer, i + 1)
                    ahead(4, 5)
                moe_steps(dve, layer, split, step)

                def overflow_dve(n, v):
                    dve.wait_ge(v["silu"], n + 1)
                    dve.wait_ge(v["used"], 6 * n + 4)
                    dve.tensor_tensor(AG[:, :], ps[1][:, :], SG[:, :], ALU.mult).then_inc(v["glu"], 1)
                overflow(dve, layer, overflow_dve)

            def combine(layer):
                for t in range(NT):
                    dve.wait_ge(y_loaded[t % 2], 16 * (2 * layer + t // 2 + 1))
                    link(dve.scalar_tensor_tensor(out=H[:, t, :], in0=Y2[:, t % 2, 0:D], scalar=w_tok[:, 0, t:t + 1],
                                                  in1=H[:, t, :], op0=ALU.mult, op1=ALU.add))
                    dve.scalar_tensor_tensor(out=H[:, t, :], in0=Y2[:, t % 2, D:2 * D], scalar=w_tok[:, 1, t:t + 1],
                                             in1=H[:, t, :], op0=ALU.mult, op1=ALU.add).then_inc(S["combined"], 1)

            def ple(layer, n, m, gain_no):
                combine(layer)
                norm_phase(n, 4, m, gain_no)
                for c in range(2):
                    split.to(PG[layer] + 2 * c + AHEAD)
                    split.to(PG[layer] + 2 * c + 1 + AHEAD)
                    for j in range(4):
                        wait_freed(dve, f"pg{layer}{c}", j)
                        at = slice(c * 512, (c + 1) * 512)
                        link(dve.tensor_tensor(GT[:, j, :], GT[:, j, :], PU[:, j, at], ALU.mult))
                        dve.tensor_tensor(H[:, j, at], H[:, j, at], GT[:, j, :], ALU.add).then_inc(S["ple_added"], 1)

            norm_phase(2, 4, 1, 2, store=0)
            split_p(0)
            route(0)
            moe(0)
            ple(0, 3, 2, 3)

            norm_phase(4, 0, 3, 4)
            dve.wait_ge(S["ws_loaded"], 16)
            dve.tensor_tensor(WST[:, :, :], WST[:, :, :], causal.unsqueeze(1).broadcast_to([P, 8, P]), ALU.mult)\
                .then_inc(S["ws_masked"], 1)
            for c in range(4):
                split.to(SV[c] + AHEAD)
                split.to(SV[c] + 1 + AHEAD)
            for t in range(NT):
                wait_freed(dve, "sv3", t)
                link(dve.tensor_reduce(vst[:, 0, t:t + 1], vsum[:, t, :], AX.X, ALU.add))
                dve.tensor_scalar(vst[:, 1, t:t + 1], vst[:, 0, t:t + 1], -1.0 / (2 * D), None, ALU.mult)\
                    .then_inc(S["mean_ready"], 1)
            def layer_norm(half):
                for t in range(NT):
                    at = VS[:, t, half * D:(half + 1) * D]
                    if half == 0:
                        dve.wait_ge(S["ln_root"], t + 1)
                        link(dve.reciprocal(vst[:, 4, t:t + 1], vst[:, 3, t:t + 1]))
                    link(dve.tensor_scalar(at, at, vst[:, 1, t:t + 1], vst[:, 4, t:t + 1], ALU.add, ALU.mult))
                    if t == 0:
                        dve.wait_ge(S["ln_loaded"], 32 * half + 32)
                    link(dve.tensor_tensor(at, at, lnG[:, :], ALU.mult))
                    dve.tensor_tensor(at, at, lnB[:, :], ALU.add).then_inc(S["ln_done"], 1)

            layer_norm(0)
            for c in range(4):
                split.to(SU[c] + AHEAD)
                split.to(SU[c] + 1 + AHEAD)
                for t in range(NT):
                    wait_freed(dve, f"su{c}", t)
                    dve.wait_ge(S["s_done"], 4 * c + t + 1)
                    for gg in range(2):
                        g = 2 * c + gg
                        dve.scalar_tensor_tensor(
                            out=VS[:, t, g * 256:(g + 1) * 256], in0=ps[t][:, gg * 256:(gg + 1) * 256],
                            scalar=small[:, S_BS + g:S_BS + g + 1], in1=UT[:, t, gg * 256:(gg + 1) * 256],
                            op0=ALU.add, op1=ALU.mult).then_inc(S["prod_done"], 1)
                if c == 0:
                    layer_norm(1)
            for half in range(2):
                for t in range(NT):
                    low(5 + half, 4 if half == 0 else 0, t)
                for c in range(2):
                    add_out(f"so{half}{c}", SO[half][c], 4 * ((half + c) % 2), c)
                    if half == 1 and c == 0:
                        split_router(1)
            norm_phase(7, 4, 4, 5, store=1)
            split_p(1)
            route(1)
            moe(1)
            ple(1, 8, 5, 6)
            for t in range(NT):
                norm(6, None, t, None, 7)

        @block.gpsimd
        def _(pool):
            copies = [0]

            def load_gain(k, ready):
                ready()
                pool.dma_start(gain[:, :], gains_in[k]).then_inc(S["gain_loaded"], 16)

            def after_rows(m):
                return lambda: pool.wait_ge(S["rows_ready"], 4 * m + 4)

            load_gain(0, lambda: None)
            load_gain(1, after_rows(0))
            load_gain(2, lambda: pool.wait_ge(S["sr_scaled"], NT))
            pool.wait_ge(S["o_gated"], NT)
            pool.dma_start(pT[:, :, :], pt_in[0]).then_inc(S["pt_loaded"], 16)
            pool.wait_ge(S["xt_pe"], 16)
            pool.dma_start(rw[:, :, :], router_in[0]).then_inc(S["rw_loaded"], 16)

            def store_rows(layer, m):
                for t in range(NT):
                    pool.wait_ge(S["rows_ready"], 4 * m + t + 1)
                    pool.dma_start(hn_dram[layer][t * P:(t + 1) * P, :], HN[:, t % 2, :]).then_inc(hn_stored[t % 2], 16)
                pool.wait_ge(S["router_done"], layer + 1)
                pool.memset(XG[:, :], 0.0).then_inc(S["xg_cleared"], 1)

            def gather(layer, e):
                q = EXPERTS * layer + e
                first = isinstance(e, int) and e == 0
                if not first:
                    pool.wait_ge(S["gx_pe"], 2 * q)
                if not (first and layer == 0):
                    pool.wait_ge(S["gathered"], 16 * q)
                col(slot_tokens, e, gather_col)
                pool.indirect_dma_start(out=XG[:, :], out_offset=None, in_=hn_dram[layer],
                                        in_offset=bass.IndirectOffsetOnAxis(ap=gather_col[:, :], axis=0),
                                        bounds_check=SEQ - 1, oob_is_err=False).then_inc(S["gathered"], 16)

            def scatter(layer, e):
                q = EXPERTS * layer + e
                pool.wait_ge(S["y_act"], q + 1)
                pool.wait_ge(S["y_dve"], q + 1)
                if not (isinstance(e, int) and e == 0 and layer == 0):
                    pool.wait_ge(S["scattered"], 16 * q)
                col(slot_rows, e, scatter_col)
                pool.indirect_dma_start(out=y_dram[layer], out_offset=bass.IndirectOffsetOnAxis(ap=scatter_col[:, :], axis=0),
                                        in_=Y[:, :], in_offset=None,
                                        bounds_check=2 * SEQ - 1, oob_is_err=False).then_inc(S["scattered"], 16)

            def col(table, c, to):
                copies[0] += 1
                pool.tensor_copy(to[:, :], table[:, c:c + 1]).then_inc(S["col_copied"], 1)
                pool.wait_ge(S["col_copied"], copies[0])

            def moe(layer, m):
                for b in range(2):
                    pool.wait_ge(hn_stored[b], 32 * layer + 32)
                pool.wait_ge(S["xg_cleared"], layer + 1)
                pool.wait_ge(S["slots_ready"], layer + 1)
                for e in range(4):
                    gather(layer, e)
                for i in range(2, EXPERTS + 2):
                    scatter(layer, i - 2)
                    if i + 2 < EXPERTS:
                        gather(layer, i + 2)
                pool.wait_ge(S["scattered"], 16 * EXPERTS * (layer + 1))
                v = OV[layer]
                pool.wait_ge(S["extra_ready"], layer + 1)
                count = pool.value_load(extra_i[0:1, 0, 0:1], min_val=0, max_val=EXTRA)
                for n in range(EXTRA):
                    with pool.If(count > n):
                        c = pool.value_load(extra_i[0:1, 1, n:n + 1], min_val=0, max_val=ROUNDS * EXPERTS - 1)
                        pool.tensor_copy(gather_col[:, :], slot_tokens[:, bass.ds(c, 1)]).then_inc(v["col"], 1)
                        pool.wait_ge(v["col"], 2 * n + 1)
                        pool.indirect_dma_start(
                            out=XG[:, :], out_offset=None, in_=hn_dram[layer],
                            in_offset=bass.IndirectOffsetOnAxis(ap=gather_col[:, :], axis=0),
                            bounds_check=SEQ - 1, oob_is_err=False).then_inc(v["gathered"], 16)
                        pool.tensor_copy(scatter_col[:, :], slot_rows[:, bass.ds(c, 1)]).then_inc(v["col"], 1)
                        pool.wait_ge(v["col"], 2 * n + 2)
                        pool.wait_ge(v["y"], 2 * n + 2)
                        pool.indirect_dma_start(
                            out=y_dram[layer],
                            out_offset=bass.IndirectOffsetOnAxis(ap=scatter_col[:, :], axis=0),
                            in_=Y[:, :], in_offset=None,
                            bounds_check=2 * SEQ - 1, oob_is_err=False).then_inc(v["scattered"], 16)
                        pool.wait_ge(v["scattered"], 16 * n + 16)
                for t in range(NT):
                    if t >= 2:
                        pool.wait_ge(S["combined"], 4 * layer + t - 1)
                    pool.dma_start(Y2[:, t % 2, :],
                                   y_dram[layer][2 * t * P:2 * (t + 1) * P, :].rearrange("(p k) d -> p (k d)", p=P))\
                        .then_inc(y_loaded[t % 2], 16)

            store_rows(0, 1)
            load_gain(3, after_rows(1))
            moe(0, 1)
            load_gain(4, after_rows(2))
            pool.wait_ge(S["ple_added"], 8)
            pool.dma_start(WST[:, :, :], ws_in).then_inc(S["ws_loaded"], 16)
            for half in range(2):
                if half:
                    pool.wait_ge(S["ln_done"], NT)
                pool.dma_start(lnG[:, :], ln_in[2 * half]).then_inc(S["ln_loaded"], 16)
                pool.dma_start(lnB[:, :], ln_in[2 * half + 1]).then_inc(S["ln_loaded"], 16)
                if half == 0:
                    load_gain(5, after_rows(3))
            pool.wait_ge(S["prod_done"], 32)
            pool.dma_start(rw[:, :, :], router_in[1]).then_inc(S["rw_loaded"], 16)
            pool.wait_ge(S["xt_pe"], 8 * 7)
            pool.dma_start(pT[:, :, :], pt_in[1]).then_inc(S["pt_loaded"], 16)
            store_rows(1, 4)
            load_gain(6, after_rows(4))
            moe(1, 4)
            load_gain(7, after_rows(5))


def _lay_out(a):
    import numpy as np
    f = {k: np.asarray(v) for k, v in a.items()}
    stream = np.empty((UNITS, P, UNIT), np.float32)
    at = [0]

    def put(w):
        stream[at[0]] = w.reshape(4, P, 512).transpose(1, 0, 2).reshape(P, UNIT)
        at[0] += 1

    def block(w, c):
        for half in range(w.shape[0] // 512):
            put(w[half * 512:(half + 1) * 512, c:c + 512])

    def moe(layer):
        stream[at[0]] = f["ple_w_up"][layer].reshape(2, P, D).transpose(1, 0, 2).reshape(P, UNIT)
        at[0] += 1
        for i in range(EXPERTS + 1):
            if i < EXPERTS:
                block(f["moe_w_gate"][layer, i], 0)
                block(f["moe_w_up"][layer, i], 0)
            if i:
                for c in (0, 512):
                    block(f["moe_w_down"][layer, i - 1], c)
        for c in (0, 512):
            block(f["ple_w_gate"][layer], c)

    w = f["gla_w_in"][0]
    for c in (1024, 0, 512, 1536, 2048, 2560):
        block(w, c)
    for c in (0, 512):
        block(f["gla_w_out"][0], c)
    moe(0)
    w = f["sgu_w_in"][0]
    for c in range(2048, 4096, 512):
        block(w, c)
    for c in range(0, 2048, 512):
        block(w, c)
    for half in range(2):
        for c in (0, 512):
            block(f["sgu_w_out"][0][half * D:(half + 1) * D], c)
    moe(1)
    assert at[0] == UNITS

    def rep(v):
        return np.broadcast_to(v, (P,) + v.shape)

    con = np.zeros((P, C_END), np.float32)
    i, j = np.arange(P)[:, None], np.arange(P)[None, :]
    con[:, C_ID:C_ID + P] = i == j
    con[:, C_ONE:C_ONE + P] = 1
    con[:, C_BEFORE:C_BEFORE + P] = i < j
    con[:, C_CHUNK:C_CHUNK + P] = (i <= j) & (i // CHUNK == j // CHUNK)
    con[:, C_CAUSAL:C_CAUSAL + P] = i <= j
    con[:, C_TIE:C_TIE + 16] = np.tile([4, 3, 2, 1], NT)
    con[:, C_EOFF:C_EOFF + 64] = np.tile(np.arange(16), NT)
    con[:, C_NUM:C_NUM + EXTRA] = np.arange(1, EXTRA + 1)
    pairs, e = np.arange(ROUNDS * EXPERTS), np.arange(ROUNDS * EXPERTS) % EXPERTS
    gate = [unit_of(0, int(k), 0) for k in e]
    down = [unit_of(0, int(k) + 1, 0 if k == EXPERTS - 1 else 4) for k in e]
    con[:, C_TAB:C_IOTA] = np.concatenate([pairs, gate, down])
    con[:, C_IOTA:C_IOTA + P] = np.arange(P)
    scan = np.tile((np.arange(SEQ) % CHUNK != 0).astype(np.float32), (P, 1))
    for t in range(NT):
        for k in range(2):
            con[:, C_ROW + k * NT + t] = 2 * (t * P + np.arange(P)) + k + 1
    small = np.zeros((P, S_END), np.float32)
    small[:, S_BG:S_BG + 4] = f["gla_b_gate"][0].reshape(4, P).T
    small[:, S_BS:S_BS + 8] = f["sgu_b_s"][0].T
    router = np.zeros((2, P, KD, P), np.float32)
    for layer in range(2):
        for t in range(NT):
            c = S_RB + 80 * layer + 20 * t
            small[:, c:c + 4] = f["moe_b_route_group"][layer]
            small[:, c + 4:c + 20] = f["moe_b_route_expert"][layer].reshape(16)
        router[layer, :, :, 0:4] = f["moe_w_route_group"][layer].reshape(KD, P, 4).transpose(1, 0, 2)
        router[layer, :, :, 4:20] = f["moe_w_route_expert"][layer].reshape(KD, P, 16).transpose(1, 0, 2)
    wa = np.zeros((P, KD, P), np.float32)
    wa[:, :, 0:16] = f["gla_w_in"][0][:, 3072:3088].reshape(KD, P, 16).transpose(1, 0, 2)
    wgu = np.zeros((P, 512), np.float32)
    wgu[0:16] = f["gla_w_gate_up"][0]
    gains = np.stack([rep(v) for v in (
        f["norm_mix_g"][0], f["gla_g_head"][0], f["norm_ffn_g"][0], f["norm_ple_g"][0],
        f["norm_mix_g"][1], f["norm_ffn_g"][1], f["norm_ple_g"][1], f["final_norm_g"])])
    ln = np.stack([rep(v) for half in range(2) for v in (
        f["sgu_ln_g"][0][half * D:(half + 1) * D], f["sgu_ln_b"][0][half * D:(half + 1) * D])])
    ws = f["sgu_w_s"][0].transpose(2, 0, 1)
    pt = np.stack([f["p"][i, 0].T.reshape(2, P, SEQ).transpose(1, 0, 2) for i in range(2)])
    x = f["x"][0].reshape(NT, P, D).transpose(1, 0, 2)
    return {"weight_stream": stream, "x": x, "constants": con, "scan": scan, "small": small,
            "gains": gains, "ln": ln, "router": router, "wa": wa, "wgu": wgu, "ws": ws, "pt": pt}


def kernel(**inputs):
    import numpy as _np
    import concourse.bacc as _bacc
    from concourse.bass_utils import run_bass_kernel_spmd as _run

    nc = _bacc.Bacc("TRN2", target_bir_lowering=False, num_devices=1)
    arrays = {f"in_{k}": _np.ascontiguousarray(v) for k, v in _lay_out(inputs).items()}
    args = [nc.dram_tensor(k, v.shape, mybir.dt.from_np(v.dtype), kind="ExternalInput").ap()
            for k, v in arrays.items()]
    out = nc.dram_tensor("out", (NT, P, D), F32, kind="ExternalOutput").ap()
    hn = [nc.dram_tensor(f"hn{i}", (SEQ, D), F32).ap() for i in range(2)]
    y = [nc.dram_tensor(f"y{i}", (2 * SEQ, D), F32).ap() for i in range(2)]
    ins = dict(zip(arrays, args))
    build(nc, ins["in_weight_stream"], ins["in_x"], ins["in_constants"], ins["in_scan"],
          ins["in_small"], ins["in_gains"], ins["in_ln"], ins["in_router"], ins["in_wa"], ins["in_wgu"],
          ins["in_ws"], ins["in_pt"], out, hn, y)
    r = _run(nc, [arrays], core_ids=[0])
    return r.results[0]["out"].reshape(1, SEQ, D)
```
